# Optimizing a Trainium2 kernel written in Bass

```python
import jax, jax.numpy as jnp
from jax import lax
import numpy as np

D_MODEL = 1024
BATCH = 1
SEQ = 256
DEPTH = 1

CHUNK = 64
Q_BLOCK = 128
EPS = 1e-6
D_ATTN = D_MODEL // 2
HEAD_DIM = 64
N_HEADS = D_ATTN // HEAD_DIM
N_IDX_HEADS = 4
IDX_DIM = 64
TOPK_MAX = 256
D_POOL = D_MODEL // 2
POOL_WINDOWS = (2, 4, 8, 16)
N_POOL_GROUPS = len(POOL_WINDOWS)
POOL_GROUP_DIM = D_POOL // N_POOL_GROUPS
N_BRANCH = 2
N_EXPERTS = 32
TOP_K_EXPERTS = 4
D_EXPERT = D_MODEL
SWIGLU_LIMIT = 7.0
SWIGLU_ALPHA = 1.702
_WIDTHS = (D_ATTN, D_ATTN, D_ATTN, N_IDX_HEADS * IDX_DIM, IDX_DIM, N_IDX_HEADS, D_POOL, N_BRANCH * D_MODEL)
D_IN_PROJ = sum(_WIDTHS)
SPLIT_OFFSETS = tuple(int(v) for v in np.cumsum(_WIDTHS)[:-1])

kernel_name = "hybrid_dsa_pool_moe_block"

def _rmsnorm(x, g):
    xf = x.astype(jnp.float32)
    xf = xf * lax.rsqrt(jnp.mean(xf * xf, axis=-1, keepdims=True) + EPS)
    return (xf * g.astype(jnp.float32)).astype(x.dtype)

def _gather_rows(kb, ib):
    return kb[ib]

def _dsa_attention(q, k, v, iq, ik, iw, q_norm_g, k_norm_g):
    B_, S_ = q.shape[0], q.shape[1]
    L = S_
    topk = min(TOPK_MAX, L // 4)
    n_blocks = S_ // Q_BLOCK
    q = _rmsnorm(q, q_norm_g)
    k = _rmsnorm(k, k_norm_g)
    scale = HEAD_DIM ** -0.5
    idx_scale = IDX_DIM ** -0.5
    iw = iw.astype(jnp.float32) * (N_IDX_HEADS ** -0.5)
    key_pos = jnp.arange(S_)

    def to_blocks(a):
        return jnp.swapaxes(a.reshape((B_, n_blocks, Q_BLOCK) + a.shape[2:]), 0, 1)

    def one_block(args):
        qb, iqb, iwb, blk = args
        t = blk * Q_BLOCK + jnp.arange(Q_BLOCK)
        limit = (t // CHUNK + 1) * CHUNK
        admissible = key_pos[None, :] < limit[:, None]
        dots = jnp.einsum('bthd,bsd->bths', iqb, ik).astype(jnp.float32) * idx_scale
        score = jnp.einsum('bths,bth->bts', jax.nn.relu(dots), iwb)
        score = jnp.where(admissible[None], score, -jnp.inf)
        _, sel = lax.top_k(score, topk)
        valid = sel < limit[None, :, None]
        ksel = jax.vmap(_gather_rows)(k, sel)
        vsel = jax.vmap(_gather_rows)(v, sel)
        logits = jnp.einsum('bthd,btkhd->bhtk', qb, ksel).astype(jnp.float32) * scale
        logits = jnp.where(valid[:, None], logits, -jnp.inf)
        p = jax.nn.softmax(logits, axis=-1)
        return jnp.einsum('bhtk,btkhd->bthd', p.astype(vsel.dtype), vsel)

    out = lax.map(one_block, (to_blocks(q), to_blocks(iq), to_blocks(iw), jnp.arange(n_blocks)))
    out = jnp.swapaxes(out, 0, 1).reshape(B_, S_, N_HEADS * HEAD_DIM)
    return out

def _pool_mixer(u, pool_w, pool_b, pool_scale):
    B_, S_, _ = u.shape
    uf = u.astype(jnp.float32)
    csum = jnp.concatenate([jnp.zeros((B_, 1, D_POOL), jnp.float32), jnp.cumsum(uf, axis=1)], axis=1)
    t = jnp.arange(S_)
    groups = []
    for g, w in enumerate(POOL_WINDOWS):
        sl = slice(g * POOL_GROUP_DIM, (g + 1) * POOL_GROUP_DIM)
        lo = jnp.maximum(t + 1 - w, 0)
        cnt = (t + 1 - lo).astype(jnp.float32)
        c = csum[:, :, sl]
        mean = (c[:, 1:] - jnp.take(c, lo, axis=1)) / cnt[None, :, None]
        groups.append(mean - uf[:, :, sl])
    y = jnp.stack(groups, axis=2).astype(u.dtype)
    y = jnp.einsum('bsgc,gcd->bsgd', y, pool_w).reshape(B_, S_, D_POOL)
    return (y + pool_b) * pool_scale

def _moe(h, router_w, router_b, w1, b1, w2, b2):
    B_, S_, D_ = h.shape
    tok = h.reshape(-1, D_)
    logits = (tok @ router_w).astype(jnp.float32) + router_b.astype(jnp.float32)
    topv, topi = lax.top_k(logits, TOP_K_EXPERTS)
    topw = jax.nn.softmax(topv, axis=-1)
    combine = jnp.sum(jax.nn.one_hot(topi, N_EXPERTS, dtype=jnp.float32) * topw[..., None], axis=1)
    out = jnp.zeros(tok.shape, jnp.float32)
    for e in range(N_EXPERTS):
        gu = tok @ w1[e] + b1[e]
        gate = jnp.minimum(gu[:, :D_EXPERT], SWIGLU_LIMIT)
        lin = jnp.clip(gu[:, D_EXPERT:], -SWIGLU_LIMIT, SWIGLU_LIMIT)
        act = (lin + 1) * gate * jax.nn.sigmoid(SWIGLU_ALPHA * gate)
        out = out + combine[:, e:e + 1] * (act @ w2[e] + b2[e])
    return out.reshape(B_, S_, D_).astype(h.dtype)

def setup_inputs(seed: int = 0) -> dict:
    key = jax.random.key(seed)
    ks = jax.random.split(key, 20)
    f32 = jnp.float32
    nrm = lambda k, shape, s: jax.random.normal(k, shape, f32) * s
    return {
        "x": nrm(ks[0], (BATCH, SEQ, D_MODEL), 1.0),
        "attn_norm_g": 1.0 + nrm(ks[1], (DEPTH, D_MODEL), 0.05),
        "w_in": nrm(ks[2], (DEPTH, D_MODEL, D_IN_PROJ), D_MODEL ** -0.5),
        "q_norm_g": 1.0 + nrm(ks[3], (DEPTH, HEAD_DIM), 0.05),
        "k_norm_g": 1.0 + nrm(ks[4], (DEPTH, HEAD_DIM), 0.05),
        "pool_w": nrm(ks[5], (DEPTH, N_POOL_GROUPS, POOL_GROUP_DIM, POOL_GROUP_DIM), POOL_GROUP_DIM ** -0.5),
        "pool_b": nrm(ks[6], (DEPTH, D_POOL), 0.02),
        "pool_scale": 1.0 + nrm(ks[7], (DEPTH, D_POOL), 0.05),
        "w_branch_attn": nrm(ks[8], (DEPTH, D_ATTN, D_MODEL), D_ATTN ** -0.5),
        "w_branch_pool": nrm(ks[9], (DEPTH, D_POOL, D_MODEL), D_POOL ** -0.5),
        "w_out": nrm(ks[10], (DEPTH, D_MODEL, D_MODEL), D_MODEL ** -0.5),
        "ffn_norm_g": 1.0 + nrm(ks[11], (DEPTH, D_MODEL), 0.05),
        "router_w": nrm(ks[12], (DEPTH, D_MODEL, N_EXPERTS), D_MODEL ** -0.5),
        "router_b": nrm(ks[13], (DEPTH, N_EXPERTS), 0.01),
        "expert_w1": nrm(ks[14], (DEPTH, N_EXPERTS, D_MODEL, 2 * D_EXPERT), D_MODEL ** -0.5),
        "expert_b1": nrm(ks[15], (DEPTH, N_EXPERTS, 2 * D_EXPERT), 0.02),
        "expert_w2": nrm(ks[16], (DEPTH, N_EXPERTS, D_EXPERT, D_MODEL), D_EXPERT ** -0.5),
        "expert_b2": nrm(ks[17], (DEPTH, N_EXPERTS, D_MODEL), 0.02),
    }

def reference(x, attn_norm_g, w_in, q_norm_g, k_norm_g, pool_w, pool_b, pool_scale,
              w_branch_attn, w_branch_pool, w_out, ffn_norm_g, router_w, router_b,
              expert_w1, expert_b1, expert_w2, expert_b2):
    B_, S_, _ = x.shape
    for l in range(DEPTH):
        h = _rmsnorm(x, attn_norm_g[l])
        proj = h @ w_in[l]
        q, k, v, iq, ik, iw, u, gates = jnp.split(proj, SPLIT_OFFSETS, axis=-1)
        q = q.reshape(B_, S_, N_HEADS, HEAD_DIM)
        k = k.reshape(B_, S_, N_HEADS, HEAD_DIM)
        v = v.reshape(B_, S_, N_HEADS, HEAD_DIM)
        iq = iq.reshape(B_, S_, N_IDX_HEADS, IDX_DIM)
        y_attn = _dsa_attention(q, k, v, iq, ik, iw, q_norm_g[l], k_norm_g[l])
        y_pool = _pool_mixer(u, pool_w[l], pool_b[l], pool_scale[l])
        g_attn, g_pool = jnp.split(jax.nn.sigmoid(gates.astype(jnp.float32)), N_BRANCH, axis=-1)
        merged = g_attn * (y_attn @ w_branch_attn[l]) + g_pool * (y_pool @ w_branch_pool[l])
        x = x + merged.astype(x.dtype) @ w_out[l]
        h2 = _rmsnorm(x, ffn_norm_g[l])
        x = x + _moe(h2, router_w[l], router_b[l], expert_w1[l], expert_b1[l], expert_w2[l], expert_b2[l])
    return x


_drawn_inputs = setup_inputs


def setup_inputs(seed=0):
    import zlib

    import numpy as np

    out = dict(_drawn_inputs(seed))
    spreads = {}
    factors = {'q_norm_g': 4.13, 'k_norm_g': 3.072, 'expert_b1': 5.503, 'expert_b2': 6.362}
    for name, (base, spread) in spreads.items():
        noise = np.random.default_rng([zlib.crc32(name.encode()), seed]).standard_normal(out[name].shape)
        drawn = base * np.exp(spread * noise) if base else spread * noise
        out[name] = __import__('jax').numpy.asarray(drawn.astype(out[name].dtype))
    for name, factor in factors.items():
        out[name] = (out[name] * factor).astype(out[name].dtype)
    return out
```

```python
from contextlib import ExitStack

import concourse.bass as bass
from concourse import mybir

F32 = mybir.dt.float32
I32 = mybir.dt.int32
U32 = mybir.dt.uint32
ALU = mybir.AluOpType
ACT = mybir.ActivationFunctionType
AX_X = mybir.AxisListType.X

P = 128
BANK = 512
EPS = 1e-6
CHUNK = 64
TOPK_MAX = 256
POOL_WINDOWS = (2, 4, 8, 16)
SWIGLU_LIMIT = 7.0
SWIGLU_ALPHA = 1.702
TOP_EXPERTS = 4
NOT_SELECTED = -1.0e30
INADMISSIBLE = -1.0e38
TAKEN = -3.0e38
SLOTS = 64
FIRST_SLOTS = 64


def block_kernel(nc, x, attn_norm_g, w_in, q_norm_g, k_norm_g, pool_w, pool_b, pool_scale,
                 w_branch_attn, w_branch_pool, w_out, ffn_norm_g, router_w, router_b,
                 expert_w1, expert_b1, expert_w2, expert_b2, out):
    _, T, D = x.shape
    HD = q_norm_g.shape[1]
    DA = w_branch_attn.shape[1]
    H = DA // HD
    G = len(POOL_WINDOWS)
    E = router_w.shape[2]
    FE = expert_w2.shape[2]
    IH, ID = 4, 64
    TT = T // P
    KD = D // P
    KA = DA // P
    TOPK = min(TOPK_MAX, T // 4)
    KEYS = [P * (tt + 1) for tt in range(TT)]
    KEY_AT = [0, KEYS[0]]
    KEYS_ALL = sum(KEYS)
    COL_IQ = 3 * DA
    COL_IK = COL_IQ + IH * ID
    COL_IW = COL_IK + ID
    COL_U = COL_IW + IH
    COL_G = COL_U + DA
    W_IDX = COL_U - COL_IQ
    assert T == 2 * P and D == 1024 and DA == BANK and HD == 64 and FE == D and E == 32
    assert P % CHUNK == 0 and 2 * CHUNK == P and TOPK == CHUNK

    (B_IDX, B_K, B_Q, B_V, B_U, B_G0) = range(6)
    B_WA, B_WP, B_WO = B_G0 + 4, B_G0 + 5, B_G0 + 6
    N_BLOCKS = B_WO + 2
    POSITIONS = 6
    W1_CHUNKS, W2_CHUNKS = 8, 4
    RING = 2 * W1_CHUNKS + W2_CHUNKS
    SLOT_W1 = (0, W1_CHUNKS + W2_CHUNKS)
    SLOT_W2 = W1_CHUNKS

    with ExitStack() as ctx:
        def sb(name, shape, dt=F32):
            return ctx.enter_context(nc.sbuf_tensor(name, shape, dt))

        def sem(name):
            return ctx.enter_context(nc.semaphore(name))

        ring = sb("ring", [P, RING, 2048])
        S0 = SLOT_W1[1]

        def scratch(slot, at, size):
            flat = ring[:, :, :].rearrange("p s n -> p (s n)")
            base = (S0 + slot) * 2048 + at
            return flat[:, base:base + size]

        hT = scratch(0, 0, KD * T).rearrange("p (k t) -> p k t", k=KD)
        kn = scratch(1, 0, TT * DA).rearrange("p (a n) -> p a n", a=TT)
        qn = scratch(1, 1024, TT * DA).rearrange("p (a n) -> p a n", a=TT)
        attn = kn
        attnT = scratch(1, 1024, KA * T).rearrange("p (k t) -> p k t", k=KA)
        qT = scratch(2, 0, KA * T).rearrange("p (k t) -> p k t", k=KA)
        kT = scratch(2, 1024, KA * T).rearrange("p (k t) -> p k t", k=KA)
        merged = scratch(2, 0, TT * D).rearrange("p (a n) -> p a n", a=TT)
        gates = scratch(3, 0, TT * 2 * D).rearrange("p (a n) -> p a n", a=TT)
        probs = scratch(5, 0, H * KEYS_ALL).rearrange("p (h n) -> p h n", h=H)
        mergedT = scratch(5, 0, KD * T).rearrange("p (k t) -> p k t", k=KD)
        probsT = scratch(6, 1024, H * KEYS_ALL)
        iqT = scratch(6, 1024, 2 * T).rearrange("p (b t) -> p b t", b=2)
        ikT = scratch(6, 1536, T)
        relu = scratch(6, 1792, IH * KEYS_ALL).rearrange("p (h n) -> p h n", h=IH)
        score = scratch(7, 1280, KEYS_ALL)
        b2_all = scratch(7, 1024, D)[0:E, :]

        xs = sb("xs", [P, TT, D])
        xn = sb("xn", [P, TT, D])
        work = sb("work", [P, 7, BANK])
        squares, diffT, pooledT, v = (work[:, 0], work[:, 1:3], work[:, 3:5], work[:, 5:7])
        diffT = diffT.rearrange("p a (b t) -> p (a b) t", b=2)
        pooledT = pooledT.rearrange("p a (b t) -> p (a b) t", b=2)
        uT = xn[:, 0, :].rearrange("p (g t) -> p g t", g=G)
        sumT = xn[:, 1, :].rearrange("p (g t) -> p g t", g=G)
        x1T = work[:, 1:5].rearrange("p a (b t) -> p a b t", b=4)
        hTe, act_e, gate_e, sig_e, lin_e, actT_e, out_e = (work[:, i] for i in range(7))
        pick = sb("pick", [P, TT, SLOTS])
        put = sb("put", [P, TT, 2 * SLOTS])
        putT = sb("putT", [P, 2, TT * P])
        bias_pick = sb("bias_pick", [P, 4, SLOTS])
        b1_rows = sb("b1_rows", [P, BANK])
        ident = sb("ident", [P, P])
        ones = sb("ones", [P, P])
        before = sb("before", [P, P])
        slot_id = sb("slot_id", [P, 2 * SLOTS])
        expert_id = sb("expert_id", [P, TOP_EXPERTS * E])
        slot_fb = expert_id
        rw = sb("rw", [P, KD, E])
        rb = sb("rb", [P, E])
        unselected = work[:, 3, 0:KEYS_ALL]
        vec_rows = sb("vec_rows", [26, P])
        vecs = sb("vecs", [P, 26])
        V_G1, V_G2, V_PB, V_PS, V_QK = 0, 8, 16, 20, 24
        pool_wsb = sb("pool_wsb", [P, G, P])
        inv_count = sb("inv_count", [P, G, 16])
        top8 = sb("top8", [P, TT, 8])
        stats = sb("stats", [P, 2, 4 * TT])
        head_ss = sb("head_ss", [P, 2 * TT, H])
        eps = sb("eps", [P, 1])
        neg_max = sb("neg_max", [P, TT, H])
        iw = sb("iw", [P, TT, IH])
        max_l = sb("max_l", [P, TT, H])
        den = sb("den", [P, TT, H])
        qk_gain = sb("qk_gain", [P, 1])
        logit = sb("logit", [P, TT, E])
        rt8 = sb("rt8", [P, TT, 8])
        ri8 = sb("ri8", [P, TT, 8], U32)
        rid = sb("rid", [P, TT, 8])
        rexp = sb("rexp", [P, TT, 8])
        rsum = sb("rsum", [P, TT, 4])
        onehot = sb("onehot", [P, 2, TOP_EXPERTS * E])
        chosen = sb("chosen", [P, TT, E])
        weight = sb("weight", [P, TT, E])
        weightT = scratch(7, 768, T)[0:E, :]
        place = sb("place", [P, TT, E])
        most = sb("most", [1, 8])
        most_i = sb("most_i", [1, 8], I32)

        bank = [ctx.enter_context(nc.psum_tensor(f"bank{i}", [P, BANK], F32)) for i in range(8)]
        acc = bank[0:4]
        ps_gate, ps_lin, ps_out, ps_gather = bank[4:8]

        x_in = [sem(f"x_in{i}") for i in range(TT)]
        small_in = sem("small_in")
        block_in = [sem(f"block_in{i}") for i in range(N_BLOCKS)]
        b2_in = sem("b2_in")
        w1_in = [[sem(f"w1_in{p}_{c}") for c in range(W1_CHUNKS)] for p in range(2)]
        w2_in = [sem(f"w2_in{c}") for c in range(W2_CHUNKS)]
        w1_used, w2_used = sem("w1_used"), sem("w2_used")
        names = """consts inv_ok ident_ok vec_row_ok vec_ps vec_ok x_sq x_rms x_norm xT_ps hT_dve hT_act
            idx_ps iw_ps idx_sb iw_sb k_ps q_ps kq_sq kq_ss kq_rms kq_norm dots_ps relu_ok topk_done
            mask_ok v_ps v_sb kT_ps kT_sb qT_ps qT_sb qk_gain_ok logit_ps masked negmax prob_ok uT_ps uT_sb sum_ok
            gate_ps gate_sb probT_ps probT_sb attn_ps rden_ok attn_ok attnT_ps attnT_sb diff_ok
            pooled_ps pooled_sb branch_ps merge_ok mergedT_ps mergedT_sb out_ps x1_ok x1_sq x1_rms
            x1n_ok x1T_ps x1T_sb rw_ok logits2_ps rt_top rt_exp rt_ok weight_ok logits2_read weightT_ps weightT_sb place_ps
            place_ok most_ok acc_init result_ok stored bias_ok""".split()
        s = {n: sem(n) for n in names}
        dve_step, act_step, pool_step = sem("dve_step"), sem("act_step"), sem("pool_step")
        pick_ok, gathered, hTe_ok, gemm1, gate_ok, sig_ok, half_ok, glu_ok = (
            sem(n) for n in "pick_ok gathered hTe_ok gemm1 gate_ok sig_ok half_ok glu_ok".split())
        put_ps, put_sb, actT_ps, actT_sb, gemm2, out_ok, scattered, lin_ok = (
            sem(n) for n in "put_ps put_sb actT_ps actT_sb gemm2 out_ok scattered lin_ok".split())
        f_w, f_pick, f_ps, f_hT, f_g1, f_gate, f_sig, f_lin, f_half, f_glu, f_actT, f_actTs, f_g2, f_out, f_done, f_slot, f_mm = (
            sem("f_" + n) for n in "w pick ps hT g1 gate sig lin half glu actT actTs g2 out done slot mm".split())

        block = ctx.enter_context(nc.Block())

        class Chain:

            def __init__(self, eng, step):
                self.eng, self.step, self.n = eng, step, 0

            def link(self, ins):
                self.n += 1
                ins.then_inc(self.step, 1)
                self.eng.wait_ge(self.step, self.n)

        def at_block(i):
            pos = i % POSITIONS
            return ring[:, 2 * pos:2 * pos + 2, :].rearrange("p s n -> p (s n)")

        def block_w(i, width, rows=KD):
            return at_block(i)[:, 0:rows * width].rearrange("p (k n) -> p k n", k=rows)

        def heads(ap):
            return ap.rearrange("p (h d) -> p h d", h=H)

        def logit_ps(tt, h):
            if tt == 0:
                return bank[2 + h % 2][:, (h // 2) * P:(h // 2 + 1) * P]
            return bank[(4 if h % 2 == 0 else 0) + h // 4][:, (h // 2 % 2) * T:(h // 2 % 2 + 1) * T]

        def prob(tt, h):
            return probs[:, h, KEY_AT[tt]:KEY_AT[tt] + KEYS[tt]]

        PROB_JOBS = [[(0, 4 * j + i, 0) for i in range(4)] for j in range(2)] + [
            [(1, 2 * j + i // 2, i % 2) for i in range(4)] for j in range(4)]
        PROB_AT = {u: BANK * j + P * i for j, job in enumerate(PROB_JOBS) for i, u in enumerate(job)}
        GATE_BANK = [2, 3, 4, 5]

        def w1_slot(parity, c):
            return ring[:, SLOT_W1[parity] + c, :]

        def w2_slot(c):
            return ring[:, SLOT_W2 + c, :]

        def w1_dram(e, c):
            return expert_w1[0][bass.ds(e, 1), c * P:(c + 1) * P, :].rearrange("a p n -> p (a n)")

        def w2_dram(e, c):
            return expert_w2[0][bass.ds(e, 1), c * 2 * P:(c + 1) * 2 * P, :].rearrange(
                "a (k p) n -> p (a k) n", p=P)

        PASSES = -(-(T - FIRST_SLOTS) // SLOTS)
        PASS_DMAS = W1_CHUNKS + W2_CHUNKS

        def gather(pe):
            for k in range(KD):
                for tt in range(TT):
                    mm = pe.matmul(ps_gather[:, k * SLOTS:(k + 1) * SLOTS], xn[:, tt, k * P:(k + 1) * P],
                                   pick[:, tt, :], start=(tt == 0), stop=(tt == TT - 1))
            return mm

        def transpose_put(pe):
            for tt in range(TT):
                mm = pe.transpose(ps_lin[:, tt * P:(tt + 1) * P], put[:, tt, :], ident[:, :])
            return mm

        def up_bias(pe):
            for q in range(4):
                dst = (ps_gate, ps_lin)[q // 2][SLOTS * (q % 2):SLOTS * (q % 2 + 1), :]
                pe.matmul(dst, bias_pick[:, q, :], b1_rows[:, :], start=True, stop=False)

        def up(pe, w, k):
            for q in range(4):
                dst = (ps_gate, ps_lin)[q // 2][SLOTS * (q % 2):SLOTS * (q % 2 + 1), :]
                mm = pe.matmul(dst, hTe[:, k * SLOTS:(k + 1) * SLOTS], w[:, q * BANK:(q + 1) * BANK],
                               start=False, stop=(k == KD - 1))
            return mm

        def transpose_act(pe):
            for j in range(4):
                mm = pe.transpose(ps_gate[:, j * P:(j + 1) * P], act_e[:, j * P:(j + 1) * P], ident[:, :])
            return mm

        def down(pe, w, c):
            for k in (2 * c, 2 * c + 1):
                at = (k % 4) * P + (k // 4) * SLOTS
                for half in range(2):
                    col = (k % 2) * D + half * BANK
                    mm = pe.matmul(ps_out[SLOTS * half:SLOTS * (half + 1), :], actT_e[:, at:at + SLOTS],
                                   w[:, col:col + BANK], start=(k == 0), stop=(k == 2 * W2_CHUNKS - 1))
            return mm

        def scatter(pe, buf):
            for tt in range(TT):
                for half in range(2):
                    rows = slice(SLOTS * half, SLOTS * (half + 1))
                    mm = pe.matmul(acc[2 * tt + half][:, :], putT[rows, buf, tt * P:(tt + 1) * P], out_e[rows, :],
                                   start=False, stop=True, skip_group_check=True)
            return mm

        def build_picks(ids, e):
            for tt in range(TT):
                nc.vector.tensor_scalar(pick[:, tt, :], ids[:, 0:SLOTS], place[:, tt, bass.ds(e, 1)], None, ALU.is_equal)
                last = nc.vector.tensor_scalar(put[:, tt, :], ids[:, :], place[:, tt, bass.ds(e, 1)],
                                               weight[:, tt, bass.ds(e, 1)], ALU.is_equal, ALU.mult)
            return last

        def build_bias_pick(e):
            one = ident[:, :].rearrange("p (q e) -> p q e", q=4)[:, :, bass.ds(e, 1)]
            return nc.vector.tensor_copy(bias_pick[:, :, :], one.to_broadcast([P, 4, SLOTS]))

        def gathered_out():
            gain = vecs[:, V_G2:V_G2 + KD].rearrange("p (k a) -> p k a", a=1).to_broadcast([P, KD, SLOTS])
            return nc.vector.tensor_tensor(hTe.rearrange("p (k n) -> p k n", k=KD),
                                           ps_gather[:, :].rearrange("p (k n) -> p k n", k=KD), gain, ALU.mult)

        @block.sync
        def _(sp):
            for tt in range(TT):
                sp.dma_start(xs[:, tt, :], x[0, tt * P:(tt + 1) * P, :]).then_inc(x_in[tt], 16)

            def used(i):
                done, n = {B_IDX: (s["iw_ps"], 1), B_K: (s["k_ps"], TT), B_Q: (s["q_ps"], TT), B_V: (s["v_ps"], TT),
                           B_U: (s["uT_ps"], 2), B_WA: (s["branch_ps"], 2 * TT), B_WP: (s["branch_ps"], 2 * TT),
                           B_WO: (s["out_ps"], 2 * TT)}.get(i, (s["gate_ps"], TT * (i - B_G0 + 1)))
                sp.wait_ge(done, n)

            def load_block(i):
                if i == B_IDX:
                    dst, src = block_w(i, W_IDX), w_in[0][:, COL_IQ:COL_U]
                elif i < B_WA:
                    col = {B_K: DA, B_Q: 0, B_V: 2 * DA, B_U: COL_U}.get(i, COL_G + (i - B_G0) * BANK)
                    dst, src = block_w(i, BANK), w_in[0][:, col:col + BANK]
                elif i == B_WA:
                    dst, src = block_w(i, D, KA), w_branch_attn[0]
                elif i == B_WP:
                    dst, src = block_w(i, D, KA), w_branch_pool[0]
                else:
                    half = i - B_WO
                    dst, src = block_w(i, D, KD // 2), w_out[0][half * D // 2:(half + 1) * D // 2, :]
                if i >= POSITIONS:
                    used(i - POSITIONS)
                sp.dma_start(dst, src.rearrange("(k p) n -> p k n", p=P)).then_inc(block_in[i], 16)

            def load_w1(e, parity, c):
                sp.dma_start(w1_slot(parity, c), w1_dram(e, c)).then_inc(w1_in[parity][c], 16)

            def load_w2(e, c):
                sp.dma_start(w2_slot(c).rearrange("p (k n) -> p k n", k=2), w2_dram(e, c)).then_inc(w2_in[c], 16)

            for i in range(N_BLOCKS):
                load_block(i)
            used(B_G0 + 2)
            for c in (2, 3):
                load_w1(0, 0, c)
            used(B_G0 + 3)
            for c in (4, 5):
                load_w1(0, 0, c)
            load_w1(1, 1, 0)
            used(B_WP)
            for c in (6, 7):
                load_w1(0, 0, c)
            for c in (0, 1):
                load_w2(0, c)
            load_w1(1, 1, 1)
            sp.wait_ge(s["mergedT_ps"], 2 * TT)
            for c in (2, 3, 4):
                load_w1(1, 1, c)
            used(B_WO)
            for c in (0, 1):
                load_w1(0, 0, c)
            for c in (2, 3):
                load_w2(0, c)
            for c in (5, 6):
                load_w1(1, 1, c)
            sp.wait_ge(s["acc_init"], 1)
            load_w1(1, 1, 7)

            def expert(e, parity, more=True):
                for c in range(W2_CHUNKS):
                    if c < W2_CHUNKS - 1:
                        sp.wait_ge(w2_used, e * (W2_CHUNKS - 1) + (c + 2 - W2_CHUNKS))
                    else:
                        sp.wait_ge(gemm2, e)
                    load_w2(e, c)
                if more:
                    for c in range(W1_CHUNKS):
                        if c < W1_CHUNKS - 1:
                            sp.wait_ge(w1_used, e * (W1_CHUNKS - 1) + (c + 2 - W1_CHUNKS))
                        else:
                            sp.wait_ge(gemm1, e)
                        load_w1(e + 1, 1 - parity, c)

            with sp.Fori(0, E // 2 - 1) as i:
                expert(2 * i + 1, 1)
                expert(2 * i + 2, 0)
            expert(E - 1, 1, more=False)

            sp.wait_ge(s["most_ok"], 1)
            most_reg = sp.value_load(most_i[0:1, 0:1], min_val=0, max_val=T)
            with sp.If(most_reg > FIRST_SLOTS):
                with sp.Fori(0, PASSES) as r:
                    with sp.Fori(0, E) as e:
                        sp.wait_ge(f_done, r * E + e + 1)
                        for c in range(W1_CHUNKS):
                            sp.dma_start(w1_slot(0, c), w1_dram(e, c)).then_inc(f_w, 16)
                        for c in range(W2_CHUNKS):
                            sp.dma_start(w2_slot(c).rearrange("p (k n) -> p k n", k=2), w2_dram(e, c)).then_inc(f_w, 16)
            for tt in range(TT):
                sp.wait_ge(s["result_ok"], 2 * tt + 2)
                sp.dma_start(out[0, tt * P:(tt + 1) * P, :], xs[:, tt, :]).then_inc(s["stored"], 16)
            sp.wait_ge(s["stored"], 16 * TT)

        @block.gpsimd
        def _(pool):
            chain = Chain(pool, pool_step)
            chain.link(nc.gpsimd.memset(ident[:, :], 0.0))
            nc.gpsimd.affine_select(out=ident[:, :], in_=ident[:, :], compare_op=ALU.not_equal, fill=1.0,
                                    base=0, pattern=[[-1, P]], channel_multiplier=1).then_inc(s["ident_ok"], 1)
            chain.link(nc.gpsimd.memset(ones[:, :], 1.0))
            nc.gpsimd.affine_select(out=before[:, :], in_=ones[:, :], compare_op=ALU.is_gt, fill=0.0,
                                    base=0, pattern=[[1, P]], channel_multiplier=-1).then_inc(s["consts"], 1)
            nc.gpsimd.iota(slot_id[:, :], [[0, 2], [1, SLOTS]], base=1, channel_multiplier=0,
                           allow_small_or_imprecise_dtypes=True).then_inc(s["consts"], 1)
            nc.gpsimd.iota(expert_id[:, :], [[0, TOP_EXPERTS], [1, E]], base=0, channel_multiplier=0,
                           allow_small_or_imprecise_dtypes=True).then_inc(s["consts"], 1)
            chain.link(nc.gpsimd.iota(inv_count[:, :, :], [[0, G], [1, 16]], base=1, channel_multiplier=0,
                                      allow_small_or_imprecise_dtypes=True))
            for g, w in enumerate(POOL_WINDOWS):
                nc.gpsimd.tensor_scalar_min(inv_count[:, g, :], inv_count[:, g, :], float(w)).then_inc(s["consts"], 1)

            pool.wait_ge(s["uT_sb"], 2)
            pool.wait_ge(s["inv_ok"], 1)
            src = uT
            for j in range(G):
                dst = (sumT, diffT)[j % 2]
                sh, w = 1 << j, POOL_WINDOWS[j]
                nc.gpsimd.tensor_copy(dst[:, j:G, 0:sh], src[:, j:G, 0:sh]).then_inc(pool_step, 1)
                chain.n += 1
                chain.link(nc.gpsimd.tensor_tensor(dst[:, j:G, sh:T], src[:, j:G, sh:T], src[:, j:G, 0:T - sh], ALU.add))
                nc.gpsimd.tensor_tensor(diffT[:, j, 0:w], dst[:, j, 0:w], inv_count[:, j, 0:w], ALU.mult).then_inc(pool_step, 1)
                chain.n += 1
                chain.link(nc.gpsimd.tensor_scalar_mul(diffT[:, j, w:T], dst[:, j, w:T], 1.0 / w))
                nc.gpsimd.tensor_tensor(diffT[:, j, :], diffT[:, j, :], uT[:, j, :], ALU.subtract).then_inc(s["diff_ok"], 1)
                src = dst

        @block.scalar
        def _(act):
            chain = Chain(act, act_step)
            for row, src, n in ((V_G1, attn_norm_g, 8), (V_G2, ffn_norm_g, 8), (V_PB, pool_b, 4), (V_PS, pool_scale, 4)):
                act.dma_start(vec_rows[row:row + n, :], src[0].rearrange("(k p) -> k p", p=P)).then_inc(s["vec_row_ok"], 16)
            for h in range(2):
                act.dma_start(vec_rows[V_QK:V_QK + 1, h * HD:(h + 1) * HD], q_norm_g).then_inc(s["vec_row_ok"], 16)
                act.dma_start(vec_rows[V_QK + 1:V_QK + 2, h * HD:(h + 1) * HD], k_norm_g).then_inc(s["vec_row_ok"], 16)
            act.dma_start(rw[:, :, :], router_w[0].rearrange("(k p) n -> p k n", p=P)).then_inc(small_in, 16)
            act.dma_start(rb[:, :], router_b.to_broadcast([P, E])).then_inc(small_in, 16)
            for q in range(4):
                act.dma_start(b1_rows[E * q:E * (q + 1), :], expert_b1[0][:, q * BANK:(q + 1) * BANK]).then_inc(small_in, 16)
            act.dma_start(pool_wsb[:, :, :], pool_w[0].rearrange("g c d -> c g d")).then_inc(small_in, 16)
            act.wait_ge(s["vec_ok"], 1)
            for tt in range(TT):
                act.wait_ge(x_in[tt], 16)
                chain.link(nc.scalar.activation(work[:, 1 + 2 * tt:3 + 2 * tt, :].rearrange("p a n -> p (a n)"), xs[:, tt, :],
                                                ACT.Square, accum_out=stats[:, 0, tt:tt + 1]))
                nc.scalar.activation(stats[:, 0, TT + tt:TT + tt + 1], stats[:, 0, tt:tt + 1], ACT.Sqrt,
                                     bias=eps[:, 0:1], scale=1.0 / D).then_inc(s["x_rms"], 1)
            act.wait_ge(s["vec_ok"], 2)
            for tt in range(TT):
                act.wait_ge(s["xT_ps"], 2 * tt + 2)
                for j in range(4):
                    k = 4 + j
                    nc.scalar.activation(hT[:, k, tt * P:(tt + 1) * P], bank[2 * tt + 1][:, j * P:(j + 1) * P], ACT.Copy,
                                         scale=vecs[:, V_G1 + k:V_G1 + k + 1]).then_inc(s["hT_act"], 1)
            act.wait_ge(s["idx_ps"], 1)
            nc.scalar.copy(iqT[:, :, :], bank[4][:, :].rearrange("p (b t) -> p b t", b=2)).then_inc(s["idx_sb"], 1)
            act.wait_ge(s["idx_ps"], 2)
            nc.scalar.copy(ikT, bank[5][:, 0:T]).then_inc(s["idx_sb"], 1)
            act.wait_ge(s["iw_ps"], 1)
            nc.scalar.mul(iw[:, :, :], bank[6][:, 0:TT * IH].rearrange("p (a h) -> p a h", a=TT), IH ** -0.5).then_inc(s["iw_sb"], 1)

            def square_heads(n, src):
                if n:
                    act.wait_ge(s["kq_ss"], n)
                nc.scalar.activation(squares, src, ACT.Square).then_inc(s["kq_sq"], 1)
                act.wait_ge(s["kq_ss"], n + 1)
                nc.scalar.activation(head_ss[:, n, :], head_ss[:, n, :], ACT.Sqrt, bias=eps[:, 0:1],
                                     scale=1.0 / HD).then_inc(s["kq_rms"], 1)

            for tt in range(TT):
                act.wait_ge(s["k_ps"], tt + 1)
                square_heads(tt, bank[tt][:, :])
            for tt in range(TT):
                act.wait_ge(s["dots_ps"], tt + 1)
                for r in range(2):
                    src = bank[2 + 2 * tt + r][:, 0:2 * KEYS[tt]].rearrange("p (b n) -> p b n", b=2)
                    dst = relu[:, r:IH:2, KEY_AT[tt]:KEY_AT[tt] + KEYS[tt]]
                    nc.scalar.activation(dst, src, ACT.Relu, scale=ID ** -0.5).then_inc(s["relu_ok"], 1)
            for tt in range(TT):
                act.wait_ge(s["q_ps"], tt + 1)
                square_heads(TT + tt, bank[6 + tt][:, :])
            for tt in range(TT):
                act.wait_ge(s["v_ps"], tt + 1)
                nc.scalar.copy(v[:, tt, :], bank[2 + tt][:, :]).then_inc(s["v_sb"], 1)
            for tt in range(TT):
                act.wait_ge(s["kT_ps"], tt + 1)
                nc.scalar.copy(kT[:, :, tt * P:(tt + 1) * P], bank[tt][:, :].rearrange("p (k t) -> p k t", k=KA)).then_inc(s["kT_sb"], 1)
            for b in range(2):
                act.wait_ge(s["uT_ps"], b + 1)
                nc.scalar.copy(uT[:, 2 * b:2 * b + 2, :], bank[6 + b][:, :].rearrange("p (g t) -> p g t", g=2)).then_inc(s["uT_sb"], 1)
            for tt in range(TT):
                act.wait_ge(s["negmax"], tt + 1)
                for h in range(H):
                    nc.scalar.activation(prob(tt, h), prob(tt, h), ACT.Exp, bias=neg_max[:, tt, h:h + 1],
                                         accum_out=den[:, tt, h:h + 1]).then_inc(s["prob_ok"], 1)

            def sigmoids(c):
                for tt in range(TT):
                    n = TT * c + tt
                    act.wait_ge(s["gate_ps"], n + 1)
                    nc.scalar.activation(gates[:, tt, c * BANK:(c + 1) * BANK], bank[GATE_BANK[n % 4]][:, :],
                                         ACT.Sigmoid).then_inc(s["gate_sb"], 1)

            def probT_out(j):
                act.wait_ge(s["probT_ps"], j + 1)
                nc.scalar.copy(probsT[:, j * BANK:(j + 1) * BANK], bank[6 + j % 2][:, :]).then_inc(s["probT_sb"], 1)

            sigmoids(0)
            probT_out(0)
            probT_out(1)
            sigmoids(1)
            for j in range(2, 6):
                probT_out(j)
            sigmoids(2)
            for b in range(2):
                act.wait_ge(s["pooled_ps"], b + 1)
                for g in (2 * b, 2 * b + 1):
                    chain.link(nc.scalar.activation(pooledT[:, g, :], bank[b][:, (g % 2) * T:(g % 2 + 1) * T], ACT.Identity,
                                                    bias=vecs[:, V_PB + g:V_PB + g + 1]))
                    nc.scalar.activation(pooledT[:, g, :], pooledT[:, g, :], ACT.Copy,
                                         scale=vecs[:, V_PS + g:V_PS + g + 1]).then_inc(s["pooled_sb"], 1)
            sigmoids(3)
            for j in range(2 * TT):
                act.wait_ge(s["mergedT_ps"], j + 1)
                tt, half = j // 2, j % 2
                nc.scalar.copy(mergedT[:, 4 * half:4 * half + 4, tt * P:(tt + 1) * P],
                               bank[6 + half][:, :].rearrange("p (k t) -> p k t", k=4)).then_inc(s["mergedT_sb"], 1)
            act.wait_ge(s["attn_ps"], TT)
            act.dma_start(b2_all, expert_b2[0]).then_inc(b2_in, 16)
            for tt in range(TT):
                act.wait_ge(s["x1_ok"], 2 * tt + 2)
                chain.link(nc.scalar.activation(work[:, 5:7, :].rearrange("p a n -> p (a n)"), xs[:, tt, :],
                                                ACT.Square, accum_out=stats[:, 1, tt:tt + 1]))
                nc.scalar.activation(stats[:, 1, TT + tt:TT + tt + 1], stats[:, 1, tt:tt + 1], ACT.Sqrt,
                                     bias=eps[:, 0:1], scale=1.0 / D).then_inc(s["x1_rms"], 1)
                for b in range(2):
                    act.wait_ge(s["x1T_ps"], 2 * tt + b + 1)
                    nc.scalar.copy(x1T[:, 2 * tt + b, :, :], bank[4 + 2 * tt + b][:, :].rearrange("p (k t) -> p k t", k=4)).then_inc(s["x1T_sb"], 1)
            for tt in range(TT):
                act.wait_ge(s["rt_top"], tt + 1)
                nc.scalar.activation(rexp[:, tt, 0:TOP_EXPERTS], rt8[:, tt, 0:TOP_EXPERTS], ACT.Exp,
                                     bias=rsum[:, tt, 0:1], accum_out=rsum[:, tt, 1:2]).then_inc(s["rt_exp"], 1)

            def expert(e):
                act.wait_ge(gate_ok, e + 1)
                nc.scalar.activation(sig_e, gate_e, ACT.Sigmoid, scale=SWIGLU_ALPHA).then_inc(sig_ok, 1)
                act.wait_ge(actT_ps, e + 1)
                nc.scalar.copy(actT_e, ps_gate[:, :]).then_inc(actT_sb, 1)
                act.wait_ge(gemm2, e + 1)
                nc.scalar.copy(out_e, ps_out[:, :]).then_inc(out_ok, 1)

            with act.Fori(0, E) as e:
                expert(e)

            act.wait_ge(s["most_ok"], 1)
            most_reg = act.value_load(most_i[0:1, 0:1], min_val=0, max_val=T)
            with act.If(most_reg > FIRST_SLOTS):
                with act.Fori(0, PASSES * E) as n:
                    act.wait_ge(f_gate, n + 1)
                    nc.scalar.activation(sig_e, gate_e, ACT.Sigmoid, scale=SWIGLU_ALPHA).then_inc(f_sig, 1)
                    act.wait_ge(f_actT, n + 1)
                    nc.scalar.copy(actT_e, ps_gate[:, :]).then_inc(f_actTs, 1)
                    act.wait_ge(f_g2, n + 1)
                    nc.scalar.copy(out_e, ps_out[:, :]).then_inc(f_out, 1)

        @block.vector
        def _(dve):
            chain = Chain(dve, dve_step)
            nc.vector.memset(eps[:, :], EPS).then_inc(s["vec_ok"], 1)
            dve.wait_ge(s["vec_ps"], 1)
            nc.vector.tensor_copy(vecs[:, :], ps_out[:, 0:26]).then_inc(s["vec_ok"], 1)
            for tt in range(TT):
                dve.wait_ge(s["x_rms"], tt + 1)
                chain.link(nc.vector.reciprocal(stats[:, 0, TT + tt:TT + tt + 1], stats[:, 0, TT + tt:TT + tt + 1]))
                nc.vector.tensor_scalar(xn[:, tt, :], xs[:, tt, :], stats[:, 0, TT + tt:TT + tt + 1], None, ALU.mult).then_inc(s["x_norm"], 1)
            dve.wait_ge(s["vec_ok"], 2)
            for tt in range(TT):
                dve.wait_ge(s["xT_ps"], 2 * tt + 1)
                gain = vecs[:, V_G1:V_G1 + 4].rearrange("p (k a) -> p k a", a=1).to_broadcast([P, 4, P])
                nc.vector.tensor_tensor(hT[:, 0:4, tt * P:(tt + 1) * P], bank[2 * tt][:, :].rearrange("p (k t) -> p k t", k=4),
                                        gain, ALU.mult).then_inc(s["hT_dve"], 1)
            dve.wait_ge(s["consts"], 3 + G)
            nc.vector.reciprocal(inv_count[:, :, :], inv_count[:, :, :]).then_inc(s["inv_ok"], 1)
            chain.link(nc.vector.tensor_tensor(qk_gain[:, :], vecs[:, V_QK:V_QK + 1], vecs[:, V_QK + 1:V_QK + 2], ALU.mult))
            chain.link(nc.vector.tensor_scalar(qk_gain[:, :], qk_gain[:, :], HD ** -0.5, None, ALU.mult))

            def norm_heads(n, src, dst):
                dve.wait_ge(s["kq_sq"], n + 1)
                nc.vector.tensor_reduce(head_ss[:, n, :], heads(squares), AX_X, ALU.add).then_inc(s["kq_ss"], 1)
                dve.wait_ge(s["kq_rms"], n + 1)
                chain.link(nc.vector.reciprocal(head_ss[:, n, :], head_ss[:, n, :]))
                inv = head_ss[:, n, :].rearrange("p (h a) -> p h a", a=1).to_broadcast([P, H, HD])
                nc.vector.tensor_tensor(heads(dst), heads(src), inv, ALU.mult).then_inc(s["kq_norm"], 1)

            for tt in range(TT):
                norm_heads(tt, bank[tt][:, :], kn[:, tt, :])
            dve.wait_ge(s["iw_sb"], 1)
            for tt in range(TT):
                keys = slice(KEY_AT[tt], KEY_AT[tt] + KEYS[tt])
                dve.wait_ge(s["relu_ok"], 2 * tt + 2)
                chain.link(nc.vector.tensor_scalar(score[:, keys], relu[:, 0, keys], iw[:, tt, 0:1], None, ALU.mult))
                for h in range(1, IH):
                    chain.link(nc.vector.scalar_tensor_tensor(out=score[:, keys], in0=relu[:, h, keys], scalar=iw[:, tt, h:h + 1],
                                                              in1=score[:, keys], op0=ALU.mult, op1=ALU.add))
                chain.link(nc.vector.memset(score[0:CHUNK, keys.stop - CHUNK:keys.stop], INADMISSIBLE))
                for _ in range(TOPK // 8):
                    chain.link(nc.vector.max(top8[:, tt, :], score[:, keys]))
                    chain.link(nc.vector.match_replace(out=score[:, keys], in_to_replace=top8[:, tt, :],
                                                       in_values=score[:, keys], imm_value=TAKEN))
            nc.vector.tensor_scalar(unselected, score, (TAKEN + INADMISSIBLE) / 2, NOT_SELECTED,
                                    ALU.is_gt, ALU.mult).then_inc(s["mask_ok"], 1)
            for tt in range(TT):
                norm_heads(TT + tt, bank[6 + tt][:, :], qn[:, tt, :])
            for tt in range(TT):
                dve.wait_ge(s["qT_ps"], tt + 1)
                nc.vector.tensor_scalar(qT[:, :, tt * P:(tt + 1) * P], bank[6 + tt][:, :].rearrange("p (k t) -> p k t", k=KA),
                                        qk_gain[:, 0:1], None, ALU.mult).then_inc(s["qT_sb"], 1)
            dve.wait_ge(s["mask_ok"], 1)
            for tt in range(TT):
                dve.wait_ge(s["logit_ps"], tt + 1)
                for h in range(H):
                    nc.vector.tensor_tensor_reduce(
                        out=prob(tt, h), in0=logit_ps(tt, h), in1=unselected[:, KEY_AT[tt]:KEY_AT[tt] + KEYS[tt]],
                        scale=1.0, scalar=TAKEN, op0=ALU.add, op1=ALU.max, accum_out=max_l[:, tt, h:h + 1]).then_inc(s["masked"], 1)
                dve.wait_ge(s["masked"], H * (tt + 1))
                nc.vector.tensor_scalar(neg_max[:, tt, :], max_l[:, tt, :], -1.0, None, ALU.mult).then_inc(s["negmax"], 1)
            dve.wait_ge(small_in, 16 * 7)
            gain = vecs[:, V_G2:V_G2 + KD].rearrange("p (k a) -> p k a", a=1).to_broadcast([P, KD, E])
            nc.vector.tensor_tensor(rw[:, :, :], rw[:, :, :], gain, ALU.mult).then_inc(s["rw_ok"], 1)
            for tt in range(TT):
                dve.wait_ge(s["prob_ok"], H * (tt + 1))
                chain.link(nc.vector.reciprocal(den[:, tt, :], den[:, tt, :]))
                dve.wait_ge(s["attn_ps"], tt + 1)
                inv = den[:, tt, :].rearrange("p (h a) -> p h a", a=1).to_broadcast([P, H, HD])
                nc.vector.tensor_tensor(heads(attn[:, tt, :]), heads(bank[tt][:, :]), inv, ALU.mult).then_inc(s["attn_ok"], 1)
            for tt in range(TT):
                dve.wait_ge(s["attnT_ps"], tt + 1)
                nc.vector.tensor_copy(attnT[:, :, tt * P:(tt + 1) * P], bank[6 + tt][:, :].rearrange("p (k t) -> p k t", k=KA)).then_inc(s["attnT_sb"], 1)
            dve.wait_ge(s["gate_sb"], 4 * TT)
            for j in range(2 * TT):
                tt, half = j // 2, j % 2
                cols = slice(half * BANK, (half + 1) * BANK)
                g_p = gates[:, tt, D + half * BANK:D + (half + 1) * BANK]
                dve.wait_ge(s["branch_ps"], j + 1)
                nc.vector.tensor_tensor(merged[:, tt, cols], bank[2 + 2 * (j % 2)][:, :], gates[:, tt, cols], ALU.mult).then_inc(dve_step, 1)
                chain.n += 1
                chain.link(nc.vector.tensor_tensor(g_p, bank[3 + 2 * (j % 2)][:, :], g_p, ALU.mult))
                nc.vector.tensor_tensor(merged[:, tt, cols], merged[:, tt, cols], g_p, ALU.add).then_inc(s["merge_ok"], 1)
            for j in range(2 * TT):
                tt, half = j // 2, j % 2
                cols = slice(half * BANK, (half + 1) * BANK)
                dve.wait_ge(s["out_ps"], j + 1)
                nc.vector.tensor_tensor(xs[:, tt, cols], xs[:, tt, cols], bank[j][:, :], ALU.add).then_inc(s["x1_ok"], 1)
            for tt in range(TT):
                dve.wait_ge(s["x1_rms"], tt + 1)
                chain.link(nc.vector.reciprocal(stats[:, 1, TT + tt:TT + tt + 1], stats[:, 1, TT + tt:TT + tt + 1]))
                rstd = stats[:, 1, TT + tt:TT + tt + 1]
                nc.vector.tensor_scalar(xn[:, tt, :], xs[:, tt, :], rstd, None, ALU.mult).then_inc(s["x1n_ok"], 1)
                dve.wait_ge(s["logits2_ps"], tt + 1)
                nc.vector.scalar_tensor_tensor(out=logit[:, tt, :], in0=bank[6][:, tt * E:(tt + 1) * E] if tt else bank[7][:, 0:E],
                                                          scalar=rstd, in1=rb[:, :], op0=ALU.mult, op1=ALU.add).then_inc(s["logits2_read"], 1)
                dve.wait_ge(s["logits2_read"], tt + 1)
                chain.link(nc.vector.max(rt8[:, tt, :], logit[:, tt, :]))
                nc.vector.tensor_scalar(rsum[:, tt, 0:1], rt8[:, tt, 0:1], -1.0, None, ALU.mult).then_inc(s["rt_top"], 1)
                chain.link(nc.vector.max_index(out=ri8[:, tt, :], in_max=rt8[:, tt, :], in_values=logit[:, tt, :]))
                chain.link(nc.vector.tensor_copy(rid[:, tt, :], ri8[:, tt, :]))
                hot = onehot[:, 0, :].rearrange("p (k e) -> p k e", k=TOP_EXPERTS)
                weighted = onehot[:, 1, :].rearrange("p (k e) -> p k e", k=TOP_EXPERTS)
                ids = rid[:, tt, 0:TOP_EXPERTS].rearrange("p (k a) -> p k a", a=1).to_broadcast([P, TOP_EXPERTS, E])
                chain.link(nc.vector.tensor_tensor(hot, expert_id[:, :].rearrange("p (k e) -> p k e", k=TOP_EXPERTS), ids, ALU.is_equal))
                nc.vector.tensor_reduce(chosen[:, tt, :], onehot[:, 0, :].rearrange("p (k e) -> p e k", k=TOP_EXPERTS), AX_X, ALU.add).then_inc(s["rt_ok"], 1)
                dve.wait_ge(s["rt_exp"], tt + 1)
                chain.link(nc.vector.reciprocal(rsum[:, tt, 2:3], rsum[:, tt, 1:2]))
                chain.link(nc.vector.tensor_scalar(rexp[:, tt, 0:TOP_EXPERTS], rexp[:, tt, 0:TOP_EXPERTS], rsum[:, tt, 2:3], None, ALU.mult))
                share = rexp[:, tt, 0:TOP_EXPERTS].rearrange("p (k a) -> p k a", a=1).to_broadcast([P, TOP_EXPERTS, E])
                chain.link(nc.vector.tensor_tensor(weighted, hot, share, ALU.mult))
                nc.vector.tensor_reduce(weight[:, tt, :], onehot[:, 1, :].rearrange("p (k e) -> p e k", k=TOP_EXPERTS), AX_X, ALU.add).then_inc(s["weight_ok"], 1)
            dve.wait_ge(s["place_ps"], 1)
            for tt in range(TT):
                nc.vector.scalar_tensor_tensor(out=place[:, tt, :], in0=ps_out[:, tt * E:(tt + 1) * E], scalar=1.0,
                                               in1=chosen[:, tt, :], op0=ALU.add, op1=ALU.mult).then_inc(s["place_ok"], 1)
            chain.link(nc.vector.tensor_reduce(most[0:1, 0:1], ps_out[0:1, 2 * E:3 * E], AX_X, ALU.max))
            nc.vector.tensor_copy(most_i[0:1, 0:1], most[0:1, 0:1]).then_inc(s["most_ok"], 1)
            dve.wait_ge(s["weightT_ps"], 1)
            nc.vector.tensor_copy(weightT[:, :], ps_lin[0:E, 0:T]).then_inc(s["weightT_sb"], 1)
            nc.vector.tensor_scalar(slot_fb[:, :], slot_id[:, :], float(FIRST_SLOTS - SLOTS), None, ALU.add).then_inc(f_slot, 1)
            if FIRST_SLOTS < SLOTS:
                nc.vector.memset(slot_id[:, :].rearrange("p (a n) -> p a n", a=2)[:, :, FIRST_SLOTS:SLOTS], -1.0).then_inc(f_slot, 1)
                dve.wait_ge(f_slot, 2)
            dve.wait_ge(s["place_ok"], TT)
            build_picks(slot_id, 0).then_inc(pick_ok, 1)

            def expert(e, buf, more=True, more2=True):
                dve.wait_ge(gemm1, e + 1)
                nc.vector.tensor_scalar(gate_e, ps_gate[:, :], SWIGLU_LIMIT, None, ALU.min).then_inc(gate_ok, 1)
                nc.vector.tensor_scalar(lin_e, ps_lin[:, :], SWIGLU_LIMIT, -SWIGLU_LIMIT, ALU.min, ALU.max).then_inc(lin_ok, 1)
                dve.wait_ge(gate_ok, e + 1)
                dve.wait_ge(lin_ok, e + 1)
                nc.vector.scalar_tensor_tensor(out=lin_e, in0=lin_e, scalar=1.0, in1=gate_e, op0=ALU.add,
                                               op1=ALU.mult).then_inc(half_ok, 1)
                dve.wait_ge(half_ok, e + 1)
                dve.wait_ge(sig_ok, e + 1)
                nc.vector.tensor_tensor(act_e, lin_e, sig_e, ALU.mult).then_inc(glu_ok, 1)
                if more:
                    following(e + 1, 1 - buf, more2)

            def following(e, buf, more):
                dve.wait_ge(gathered, e + 1)
                gathered_out().then_inc(hTe_ok, 1)
                build_bias_pick(e).then_inc(s["bias_ok"], 1)
                dve.wait_ge(put_ps, e + 1)
                nc.vector.tensor_copy(putT[:, buf, :], ps_lin[:, 0:TT * P]).then_inc(put_sb, 1)
                if more:
                    build_picks(slot_id, e + 1).then_inc(pick_ok, 1)

            following(0, 0, True)
            expert(0, 0)
            with dve.Fori(0, E // 2 - 2) as i:
                expert(2 * i + 1, 1)
                expert(2 * i + 2, 0)
            expert(E - 3, 1)
            expert(E - 2, 0, more2=False)
            expert(E - 1, 1, more=False)

            dve.wait_ge(f_done, 1)
            most_reg = dve.value_load(most_i[0:1, 0:1], min_val=0, max_val=T)
            with dve.If(most_reg > FIRST_SLOTS):
                with dve.Fori(0, PASSES) as r:
                    dve.wait_ge(f_done, r * E + 1)
                    nc.vector.tensor_scalar(slot_fb[:, :], slot_fb[:, :], float(SLOTS), None, ALU.add).then_inc(f_mm, 1)
                    with dve.Fori(0, E) as e:
                        n = r * E + e
                        dve.wait_ge(f_mm, r + 1)
                        dve.wait_ge(f_done, n + 1)
                        build_bias_pick(e)
                        build_picks(slot_fb, e).then_inc(f_pick, 1)
                        dve.wait_ge(f_ps, n + 1)
                        nc.vector.tensor_copy(putT[:, 0, :], ps_lin[:, 0:TT * P])
                        gathered_out().then_inc(f_hT, 1)
                        dve.wait_ge(f_g1, n + 1)
                        nc.vector.tensor_scalar(gate_e, ps_gate[:, :], SWIGLU_LIMIT, None, ALU.min).then_inc(f_gate, 1)
                        nc.vector.tensor_scalar(lin_e, ps_lin[:, :], SWIGLU_LIMIT, -SWIGLU_LIMIT, ALU.min, ALU.max).then_inc(f_lin, 1)
                        dve.wait_ge(f_gate, n + 1)
                        dve.wait_ge(f_lin, n + 1)
                        nc.vector.scalar_tensor_tensor(out=lin_e, in0=lin_e, scalar=1.0, in1=gate_e, op0=ALU.add,
                                                       op1=ALU.mult).then_inc(f_half, 1)
                        dve.wait_ge(f_half, n + 1)
                        dve.wait_ge(f_sig, n + 1)
                        nc.vector.tensor_tensor(act_e, lin_e, sig_e, ALU.mult).then_inc(f_glu, 1)
                dve.wait_ge(f_done, PASSES * E + 1)
            for j in range(2 * TT):
                tt, half = j // 2, j % 2
                cols = slice(half * BANK, (half + 1) * BANK)
                nc.vector.tensor_tensor(xs[:, tt, cols], xs[:, tt, cols], acc[j][:, :], ALU.add).then_inc(s["result_ok"], 1)

        @block.tensor
        def _(pe):
            pe.wait_ge(s["ident_ok"], 1)
            pe.wait_ge(s["vec_row_ok"], 16 * 8)
            pe.transpose(ps_out[:, 0:26], vec_rows[:, :], ident[0:26, 0:26]).then_inc(s["vec_ps"], 1)
            for tt in range(TT):
                pe.wait_ge(s["x_norm"], tt + 1)
                for b in range(2):
                    for j in range(4):
                        mm = pe.transpose(bank[2 * tt + b][:, j * P:(j + 1) * P], xn[:, tt, (4 * b + j) * P:(4 * b + j + 1) * P], ident[:, :])
                    mm.then_inc(s["xT_ps"], 1)
            pe.wait_ge(s["hT_dve"], TT)
            pe.wait_ge(s["hT_act"], 4 * TT)
            pe.wait_ge(s["vec_ok"], 2)

            pe.wait_ge(block_in[B_IDX], 16)
            w = block_w(B_IDX, W_IDX)
            for b in range(2):
                for k in range(KD):
                    mm = pe.matmul(bank[4][:, b * T:(b + 1) * T], w[:, k, b * P:(b + 1) * P], hT[:, k, :], start=(k == 0), stop=(k == KD - 1))
            mm.then_inc(s["idx_ps"], 1)
            for k in range(KD):
                for half in range(2):
                    mm = pe.matmul(bank[5][ID * half:ID * (half + 1), 0:T], w[:, k, IH * ID:IH * ID + ID], hT[:, k, :],
                                   start=(k == 0), stop=(k == KD - 1))
            mm.then_inc(s["idx_ps"], 1)
            for tt in range(TT):
                for k in range(KD):
                    mm = pe.matmul(bank[6][:, tt * IH:(tt + 1) * IH], hT[:, k, tt * P:(tt + 1) * P], w[:, k, COL_IW - COL_IQ:W_IDX],
                                   start=(k == 0), stop=(k == KD - 1))
            mm.then_inc(s["iw_ps"], 1)

            def project(i, tt, dst, done):
                w = block_w(i, BANK)
                for k in range(KD):
                    mm = pe.matmul(dst, hT[:, k, tt * P:(tt + 1) * P], w[:, k, :], start=(k == 0), stop=(k == KD - 1))
                mm.then_inc(done, 1)

            pe.wait_ge(block_in[B_K], 16)
            for tt in range(TT):
                project(B_K, tt, bank[tt][:, :], s["k_ps"])
            pe.wait_ge(s["idx_sb"], 2)
            for tt in range(TT):
                for b in range(2):
                    for r in range(2):
                        rows = slice(ID * r, ID * (r + 1))
                        mm = pe.matmul(bank[2 + 2 * tt + r][:, b * KEYS[tt]:(b + 1) * KEYS[tt]], iqT[rows, b, tt * P:(tt + 1) * P],
                                       ikT[rows, 0:KEYS[tt]], start=True, stop=True)
                mm.then_inc(s["dots_ps"], 1)
            pe.wait_ge(s["iw_sb"], 1)
            pe.wait_ge(block_in[B_Q], 16)
            for tt in range(TT):
                project(B_Q, tt, bank[6 + tt][:, :], s["q_ps"])
            pe.wait_ge(block_in[B_V], 16)
            pe.wait_ge(s["relu_ok"], 4)
            for tt in range(TT):
                project(B_V, tt, bank[2 + tt][:, :], s["v_ps"])
            for n in range(2 * TT):
                src, dst, done = (kn, bank[n], s["kT_ps"]) if n < TT else (qn, bank[4 + n], s["qT_ps"])
                pe.wait_ge(s["kq_norm"], n + 1)
                for j in range(KA):
                    mm = pe.transpose(dst[:, j * P:(j + 1) * P], src[:, n % TT, j * P:(j + 1) * P], ident[:, :])
                mm.then_inc(done, 1)
            pe.wait_ge(s["kT_sb"], TT)
            pe.wait_ge(s["qT_sb"], TT)
            pe.wait_ge(s["v_sb"], TT)
            for tt in range(TT):
                for h in range(H):
                    rows = slice(HD * (h % 2), HD * (h % 2 + 1))
                    mm = pe.matmul(logit_ps(tt, h), qT[rows, h // 2, tt * P:(tt + 1) * P], kT[rows, h // 2, 0:KEYS[tt]],
                                   start=True, stop=True)
                mm.then_inc(s["logit_ps"], 1)
            pe.wait_ge(block_in[B_U], 16)
            w = block_w(B_U, BANK)
            for g in range(G):
                for k in range(KD):
                    mm = pe.matmul(bank[6 + g // 2][:, (g % 2) * T:(g % 2 + 1) * T], w[:, k, g * P:(g + 1) * P], hT[:, k, :],
                                   start=(k == 0), stop=(k == KD - 1))
                if g % 2:
                    mm.then_inc(s["uT_ps"], 1)

            def gate_block(c):
                pe.wait_ge(block_in[B_G0 + c], 16)
                for tt in range(TT):
                    n = TT * c + tt
                    if n >= 4:
                        pe.wait_ge(s["gate_sb"], n - 3)
                    project(B_G0 + c, tt, bank[GATE_BANK[n % 4]][:, :], s["gate_ps"])

            def transpose_probs(j):
                for i, (tt, h, kb) in enumerate(PROB_JOBS[j]):
                    mm = pe.transpose(bank[6 + j % 2][:, i * P:(i + 1) * P], prob(tt, h)[:, kb * P:(kb + 1) * P], ident[:, :])
                mm.then_inc(s["probT_ps"], 1)

            def attend(tt):
                for h in range(H):
                    for kb in range(tt + 1):
                        at = PROB_AT[(tt, h, kb)]
                        mm = pe.matmul(bank[tt][:, h * HD:(h + 1) * HD], probsT[:, at:at + P], v[:, kb, h * HD:(h + 1) * HD],
                                       start=(kb == 0), stop=(kb == tt))
                mm.then_inc(s["attn_ps"], 1)

            pe.wait_ge(s["masked"], 2 * H)
            gate_block(0)
            pe.wait_ge(s["uT_sb"], 2)
            pe.wait_ge(s["prob_ok"], H)
            transpose_probs(0)
            transpose_probs(1)
            pe.wait_ge(s["probT_sb"], 2)
            attend(0)
            gate_block(1)
            pe.wait_ge(s["prob_ok"], 2 * H)
            for j in range(2, 6):
                if j >= 4:
                    pe.wait_ge(s["probT_sb"], j - 1)
                transpose_probs(j)
            pe.wait_ge(s["probT_sb"], 6)
            attend(1)
            gate_block(2)
            for tt in range(TT):
                pe.wait_ge(s["attn_ok"], tt + 1)
                for j in range(KA):
                    mm = pe.transpose(bank[6 + tt][:, j * P:(j + 1) * P], attn[:, tt, j * P:(j + 1) * P], ident[:, :])
                mm.then_inc(s["attnT_ps"], 1)
            pe.wait_ge(small_in, 16 * 7)
            pe.wait_ge(s["diff_ok"], G)
            for g in range(G):
                mm = pe.matmul(bank[g // 2][:, (g % 2) * T:(g % 2 + 1) * T], pool_wsb[:, g, :], diffT[:, g, :], start=True, stop=True)
                if g % 2:
                    mm.then_inc(s["pooled_ps"], 1)
            gate_block(3)
            for i in (B_WA, B_WP):
                pe.wait_ge(block_in[i], 16)
            pe.wait_ge(s["attnT_sb"], TT)
            pe.wait_ge(s["pooled_sb"], G)
            pe.wait_ge(s["gate_sb"], 4 * TT)

            def branches(j):
                tt, half = j // 2, j % 2
                if j >= 2:
                    pe.wait_ge(s["merge_ok"], j - 1)
                for n, (src, i) in enumerate(((attnT, B_WA), (pooledT, B_WP))):
                    w = block_w(i, D, KA)
                    for k in range(KA):
                        mm = pe.matmul(bank[2 + 2 * (j % 2) + n][:, :], src[:, k, tt * P:(tt + 1) * P],
                                       w[:, k, half * BANK:(half + 1) * BANK], start=(k == 0), stop=(k == KA - 1))
                mm.then_inc(s["branch_ps"], 1)

            def transpose_merged(tt):
                for half in range(2):
                    pe.wait_ge(s["merge_ok"], 2 * tt + half + 1)
                    if tt:
                        pe.wait_ge(s["mergedT_sb"], half + 1)
                    else:
                        pe.wait_ge(s["attnT_sb"], TT)
                    for j in range(4):
                        mm = pe.transpose(bank[6 + half][:, j * P:(j + 1) * P], merged[:, tt, (4 * half + j) * P:(4 * half + j + 1) * P], ident[:, :])
                    mm.then_inc(s["mergedT_ps"], 1)

            def project_out(tt):
                pe.wait_ge(s["mergedT_sb"], 2 * tt + 2)
                for half in range(2):
                    for k in range(KD):
                        w = block_w(B_WO + k // 4, D, KD // 2)
                        mm = pe.matmul(bank[2 * tt + half][:, :], mergedT[:, k, tt * P:(tt + 1) * P],
                                       w[:, k % 4, half * BANK:(half + 1) * BANK], start=(k == 0), stop=(k == KD - 1))
                    mm.then_inc(s["out_ps"], 1)

            def transpose_x1(tt):
                pe.wait_ge(s["x1_ok"], 2 * tt + 2)
                for b in range(2):
                    for j in range(4):
                        mm = pe.transpose(bank[4 + 2 * tt + b][:, j * P:(j + 1) * P], xs[:, tt, (4 * b + j) * P:(4 * b + j + 1) * P], ident[:, :])
                    mm.then_inc(s["x1T_ps"], 1)

            def route(tt):
                pe.wait_ge(s["x1T_sb"], 2 * tt + 2)
                dst = bank[6][:, tt * E:(tt + 1) * E] if tt else bank[7][:, 0:E]
                for k in range(KD):
                    mm = pe.matmul(dst, x1T[:, 2 * tt + k // 4, k % 4, :], rw[:, k, :], start=(k == 0), stop=(k == KD - 1))
                mm.then_inc(s["logits2_ps"], 1)

            for j in range(3):
                branches(j)
            transpose_merged(0)
            branches(3)
            for i in (B_WO, B_WO + 1):
                pe.wait_ge(block_in[i], 16)
            pe.wait_ge(s["pooled_sb"], G)
            project_out(0)
            transpose_merged(1)
            project_out(1)
            pe.wait_ge(s["merge_ok"], 2 * TT)
            pe.wait_ge(s["rw_ok"], 1)
            transpose_x1(0)
            pe.wait_ge(s["mergedT_sb"], 2 * TT)
            route(0)
            pe.wait_ge(s["logits2_read"], 1)
            transpose_x1(1)
            route(1)
            pe.wait_ge(s["consts"], 3 + G)
            pe.wait_ge(s["rt_ok"], TT)
            pe.matmul(ps_out[:, 0:E], before[:, :], chosen[:, 0, :], start=True, stop=True)
            pe.matmul(ps_out[:, E:2 * E], ones[:, :], chosen[:, 0, :], start=True, stop=False)
            pe.matmul(ps_out[:, E:2 * E], before[:, :], chosen[:, 1, :], start=False, stop=True)
            pe.matmul(ps_out[:, 2 * E:3 * E], ones[:, :], chosen[:, 0, :], start=True, stop=False)
            pe.matmul(ps_out[:, 2 * E:3 * E], ones[:, :], chosen[:, 1, :], start=False, stop=True).then_inc(s["place_ps"], 1)
            pe.wait_ge(s["weight_ok"], TT)
            for tt in range(TT):
                mm = pe.transpose(ps_lin[0:E, tt * P:(tt + 1) * P], weight[:, tt, :], ident[:, :])
            mm.then_inc(s["weightT_ps"], 1)

            def bring(e):
                pe.wait_ge(pick_ok, e + 1)
                gather(pe).then_inc(gathered, 1)

            bring(0)
            pe.wait_ge(s["weightT_sb"], 1)
            pe.wait_ge(b2_in, 16)
            pe.wait_ge(s["x1_ok"], 2 * TT)
            transpose_put(pe).then_inc(put_ps, 1)
            for j in range(2 * TT):
                mm = pe.matmul(acc[j][:, :], weightT[:, (j // 2) * P:(j // 2 + 1) * P], b2_all[:, (j % 2) * BANK:(j % 2 + 1) * BANK],
                               start=True, stop=True, skip_group_check=True)
            mm.then_inc(s["acc_init"], 1)

            def expert(e, parity, w1_round, first=False, last=False):
                pe.wait_ge(hTe_ok, e + 1)
                pe.wait_ge(s["bias_ok"], e + 1)
                pe.wait_ge(put_sb, e + 1)
                up_bias(pe)
                for k in range(W1_CHUNKS):
                    pe.wait_ge(w1_in[parity][k], w1_round * 16)
                    mm = up(pe, w1_slot(parity, k), k)
                    if k < W1_CHUNKS - 1:
                        mm.then_inc(w1_used, 1)
                mm.then_inc(gemm1, 1)
                if not first:
                    pe.wait_ge(out_ok, e)
                    scatter(pe, 1 - parity)
                if not last:
                    bring(e + 1)
                pe.wait_ge(glu_ok, e + 1)
                transpose_act(pe).then_inc(actT_ps, 1)
                if not last:
                    transpose_put(pe).then_inc(put_ps, 1)
                pe.wait_ge(actT_sb, e + 1)
                for c in range(W2_CHUNKS):
                    pe.wait_ge(w2_in[c], e * 16 + 16)
                    mm = down(pe, w2_slot(c), c)
                    if c < W2_CHUNKS - 1:
                        mm.then_inc(w2_used, 1)
                mm.then_inc(gemm2, 1)

            expert(0, 0, 1, first=True)
            with pe.Fori(0, E // 2 - 1) as i:
                expert(2 * i + 1, 1, i + 1)
                expert(2 * i + 2, 0, i + 2)
            expert(E - 1, 1, E // 2, last=True)
            pe.wait_ge(out_ok, E)
            scatter(pe, 1).then_inc(f_done, 1)

            pe.wait_ge(s["most_ok"], 1)
            most_reg = pe.value_load(most_i[0:1, 0:1], min_val=0, max_val=T)
            with pe.If(most_reg > FIRST_SLOTS):
                with pe.Fori(0, PASSES * E) as n:
                    pe.wait_ge(f_pick, n + 1)
                    transpose_put(pe)
                    gather(pe).then_inc(f_ps, 1)
                    pe.wait_ge(f_hT, n + 1)
                    up_bias(pe)
                    pe.wait_ge(f_w, n * (16 * PASS_DMAS) + 16 * PASS_DMAS)
                    for k in range(W1_CHUNKS):
                        mm = up(pe, w1_slot(0, k), k)
                    mm.then_inc(f_g1, 1)
                    pe.wait_ge(f_glu, n + 1)
                    transpose_act(pe).then_inc(f_actT, 1)
                    pe.wait_ge(f_actTs, n + 1)
                    for c in range(W2_CHUNKS):
                        mm = down(pe, w2_slot(c), c)
                    mm.then_inc(f_g2, 1)
                    pe.wait_ge(f_out, n + 1)
                    scatter(pe, 0).then_inc(f_done, 1)


_INS = ["x", "attn_norm_g", "w_in", "q_norm_g", "k_norm_g", "pool_w", "pool_b", "pool_scale", "w_branch_attn",
        "w_branch_pool", "w_out", "ffn_norm_g", "router_w", "router_b", "expert_w1", "expert_b1", "expert_w2",
        "expert_b2"]
_OUTS = [((1, 256, 1024), "float32")]


def kernel(**inputs):
    import numpy as _np
    import concourse.bacc as _bacc
    from concourse import mybir as _mybir
    from concourse.bass_utils import run_bass_kernel_spmd as _run

    nc = _bacc.Bacc("TRN2", target_bir_lowering=False, num_devices=1)
    arrays, args = {}, []
    for name in _INS:
        a = _np.ascontiguousarray(inputs[name])
        arrays[f"in_{name}_dram"] = a
        args.append(nc.dram_tensor(f"in_{name}_dram", a.shape, _mybir.dt.from_np(a.dtype), kind="ExternalInput").ap())
    for i, (shape, dtype) in enumerate(_OUTS):
        dt = _mybir.dt.from_np(_np.dtype(dtype))
        args.append(nc.dram_tensor(f"out_{i}_dram", shape, dt, kind="ExternalOutput").ap())
    block_kernel(nc, *args)
    r = _run(nc, [arrays], core_ids=[0])
    return r.results[0]["out_0_dram"]
```

```python
from contextlib import ExitStack

import concourse.bass as bass
from concourse import mybir

F32 = mybir.dt.float32
I32 = mybir.dt.int32
U32 = mybir.dt.uint32
ALU = mybir.AluOpType
ACT = mybir.ActivationFunctionType
AX_X = mybir.AxisListType.X

P = 128
BANK = 512
EPS = 1e-6
CHUNK = 64
TOPK_MAX = 256
POOL_WINDOWS = (2, 4, 8, 16)
SWIGLU_LIMIT = 7.0
SWIGLU_ALPHA = 1.702
TOP_EXPERTS = 4
NOT_SELECTED = -1.0e30
INADMISSIBLE = -1.0e38
TAKEN = -3.0e38
SLOTS = 64
FIRST_SLOTS = 64


def block_kernel(nc, x, attn_norm_g, w_in, q_norm_g, k_norm_g, pool_w, pool_b, pool_scale,
                 w_branch_attn, w_branch_pool, w_out, ffn_norm_g, router_w, router_b,
                 expert_w1, expert_b1, expert_w2, expert_b2, out):
    _, T, D = x.shape
    HD = q_norm_g.shape[1]
    DA = w_branch_attn.shape[1]
    H = DA // HD
    G = len(POOL_WINDOWS)
    E = router_w.shape[2]
    FE = expert_w2.shape[2]
    IH, ID = 4, 64
    TT = T // P
    KD = D // P
    KA = DA // P
    TOPK = min(TOPK_MAX, T // 4)
    KEYS = [P * (tt + 1) for tt in range(TT)]
    KEY_AT = [0, KEYS[0]]
    KEYS_ALL = sum(KEYS)
    COL_IQ = 3 * DA
    COL_IK = COL_IQ + IH * ID
    COL_IW = COL_IK + ID
    COL_U = COL_IW + IH
    COL_G = COL_U + DA
    W_IDX = COL_U - COL_IQ
    assert T == 2 * P and D == 1024 and DA == BANK and HD == 64 and FE == D and E == 32
    assert P % CHUNK == 0 and 2 * CHUNK == P and TOPK == CHUNK

    (B_IDX, B_K, B_Q, B_V, B_U, B_G0) = range(6)
    B_WA, B_WP, B_WO = B_G0 + 4, B_G0 + 5, B_G0 + 6
    N_BLOCKS = B_WO + 2
    POSITIONS = 6
    W1_CHUNKS, W2_CHUNKS = 8, 4
    RING = 2 * W1_CHUNKS + W2_CHUNKS
    SLOT_W1 = (0, W1_CHUNKS + W2_CHUNKS)
    SLOT_W2 = W1_CHUNKS

    with ExitStack() as ctx:
        def sb(name, shape, dt=F32):
            return ctx.enter_context(nc.sbuf_tensor(name, shape, dt))

        def sem(name):
            return ctx.enter_context(nc.semaphore(name))

        ring = sb("ring", [P, RING, 2048])
        S0 = SLOT_W1[1]

        def scratch(slot, at, size):
            flat = ring[:, :, :].rearrange("p s n -> p (s n)")
            base = (S0 + slot) * 2048 + at
            return flat[:, base:base + size]

        hT = scratch(0, 0, KD * T).rearrange("p (k t) -> p k t", k=KD)
        kn = scratch(1, 0, TT * DA).rearrange("p (a n) -> p a n", a=TT)
        qn = scratch(1, 1024, TT * DA).rearrange("p (a n) -> p a n", a=TT)
        attn = kn
        attnT = scratch(1, 1024, KA * T).rearrange("p (k t) -> p k t", k=KA)
        qT = scratch(2, 0, KA * T).rearrange("p (k t) -> p k t", k=KA)
        kT = scratch(2, 1024, KA * T).rearrange("p (k t) -> p k t", k=KA)
        merged = scratch(2, 0, TT * D).rearrange("p (a n) -> p a n", a=TT)
        gates = scratch(3, 0, TT * 2 * D).rearrange("p (a n) -> p a n", a=TT)
        probs = scratch(5, 0, H * KEYS_ALL).rearrange("p (h n) -> p h n", h=H)
        probsT = scratch(6, 1024, H * KEYS_ALL)
        iqT = scratch(6, 1024, 2 * T).rearrange("p (b t) -> p b t", b=2)
        ikT = scratch(6, 1536, T)
        relu = scratch(6, 1792, IH * KEYS_ALL).rearrange("p (h n) -> p h n", h=IH)
        score = scratch(7, 1280, KEYS_ALL)
        iwT = score[0:IH, 0:T]

        xs = sb("xs", [P, TT, D])
        xn = sb("xn", [P, TT, D])
        work = sb("work", [P, 8, BANK])
        squares, diffT, pooledT, v = (work[:, 0], work[:, 1:3], work[:, 3:5], work[:, 5:7])
        diffT = diffT.rearrange("p a (b t) -> p (a b) t", b=2)
        pooledT = pooledT.rearrange("p a (b t) -> p (a b) t", b=2)
        uT = xn[:, 0, :].rearrange("p (g t) -> p g t", g=G)
        sumT = xn[:, 1, :].rearrange("p (g t) -> p g t", g=G)
        mergedT = [xn[:, tt, :].rearrange("p (k t) -> p k t", k=KD) for tt in range(TT)]
        x1T = work[:, 1:5].rearrange("p a (b t) -> p a b t", b=4)
        hTe, act_e, gate_e, sig_e, lin_e, actT_e = (work[:, i] for i in range(6))
        rows_e = lin_e
        out_pair = work[:, 6:8]
        b2_all = work[0:E, 5:7, :].rearrange("p a n -> p (a n)")
        pick = sb("pick", [P, TT, SLOTS])
        put = sb("put", [P, TT, 2 * SLOTS])
        putT = sb("putT", [P, TT * P])
        bias_pick = sb("bias_pick", [P, 4, SLOTS])
        b1_rows = sb("b1_rows", [P, BANK])
        ident = sb("ident", [P, P])
        ones = sb("ones", [P, P])
        before = sb("before", [P, P])
        slot_id = sb("slot_id", [P, 2 * SLOTS])
        expert_id = sb("expert_id", [P, TOP_EXPERTS * E])
        slot_fb = expert_id
        rw = sb("rw", [P, KD, E])
        rb = sb("rb", [P, E])
        unselected = work[:, 3, 0:KEYS_ALL]
        gain_rows = sb("gain_rows", [8, P])
        vec_rows = sb("vec_rows", [18, P])
        vecs = sb("vecs", [P, 26])
        V_G1, V_G2, V_PB, V_PS, V_QK = 0, 8, 16, 20, 24
        pool_wsb = sb("pool_wsb", [P, G, P])
        inv_count = sb("inv_count", [P, G, 16])
        top8 = sb("top8", [P, TT, 8])
        stats = sb("stats", [P, 2, 4 * TT])
        head_ss = sb("head_ss", [P, 2 * TT, H])
        eps = sb("eps", [P, 1])
        neg_max = sb("neg_max", [P, TT, H])
        iw = sb("iw", [P, TT, IH])
        max_l = sb("max_l", [P, TT, H])
        den = sb("den", [P, TT, H])
        qk_gain = sb("qk_gain", [P, 1])
        logit = sb("logit", [P, TT, E])
        rt8 = sb("rt8", [P, TT, 8])
        ri8 = sb("ri8", [P, TT, 8], U32)
        rid = sb("rid", [P, TT, 8])
        rexp = sb("rexp", [P, TT, 8])
        rsum = sb("rsum", [P, TT, 4])
        onehot = sb("onehot", [P, 2, TOP_EXPERTS * E])
        chosen = sb("chosen", [P, TT, E])
        weight = sb("weight", [P, TT, E])
        weightT = pool_wsb[0:E, 0:2, :].rearrange("p g d -> p (g d)")
        place = sb("place", [P, TT, E])
        most = sb("most", [1, 8])
        most_i = sb("most_i", [1, 8], I32)

        bank = [ctx.enter_context(nc.psum_tensor(f"bank{i}", [P, BANK], F32)) for i in range(8)]
        acc = bank[0:4]
        ps_gate, ps_lin, ps_out, ps_gather = bank[4:8]

        x_in = [sem(f"x_in{i}") for i in range(TT)]
        small_in = sem("small_in")
        block_in = [sem(f"block_in{i}") for i in range(N_BLOCKS)]
        b2_in = sem("b2_in")
        w1_in = [[sem(f"w1_in{p}_{c}") for c in range(W1_CHUNKS)] for p in range(2)]
        w2_in = [sem(f"w2_in{c}") for c in range(W2_CHUNKS)]
        w1_used, w2_used = sem("w1_used"), sem("w2_used")
        names = """gain_in consts inv_ok ident_ok vec_row_ok vec_ps vec_ok x_rms x_norm xT_ps hT_dve hT_act
            idx_ps iw_ps idx_sb iw_sb k_ps q_ps kq_sq kq_ss kq_rms kq_norm dots_ps relu_ok mask_ok
            v_ps v_sb kT_ps kT_sb qT_ps qT_sb logit_ps masked negmax prob_ok uT_ps uT_sb
            gate_ps gate_sb probT_ps probT_sb attn_ps attn_ok attnT_ps attnT_sb diff_ok
            pooled_ps pooled_sb branch_ps merge_ok mergedT_ps mergedT_sb out_ps x1_ok x1_rms
            x1T_ps x1T_act x1T_dve rw_ok logits2_ps rt_top rt_exp rt_ok weight_ok logits2_read
            weightT_ps weightT_sb first_pick place_ps
            place_ok most_ok result_ok stored bias_ok""".split()
        s = {n: sem(n) for n in names}
        dve_step, act_step, pool_step = sem("dve_step"), sem("act_step"), sem("pool_step")
        pick_ok, gathered, hTe_ok, gemm1, gate_ok, sig_ok, half_ok, glu_ok = (
            sem(n) for n in "pick_ok gathered hTe_ok gemm1 gate_ok sig_ok half_ok glu_ok".split())
        put_ok, put_ps, put_sb, actT_ps, actT_sb, gemm2, out_ok, out2_ok, lin_ok, rows_ok, rowsT_ps = (
            sem(n) for n in "put_ok put_ps put_sb actT_ps actT_sb gemm2 out_ok out2_ok lin_ok rows_ok rowsT_ps".split())
        acc_done = sem("acc_done")
        (f_w, f_pick, f_ps, f_hT, f_g1, f_gate, f_sig, f_lin, f_half, f_glu, f_actT, f_actTs, f_g2, f_out, f_ids,
         f_rows, f_rowsT) = (sem("f_" + n) for n in (
             "w pick ps hT g1 gate sig lin half glu actT actTs g2 out ids rows rowsT").split())

        block = ctx.enter_context(nc.Block())

        class Chain:

            def __init__(self, eng, step):
                self.eng, self.step, self.n = eng, step, 0

            def link(self, ins):
                self.n += 1
                ins.then_inc(self.step, 1)
                self.eng.wait_ge(self.step, self.n)

        def at_block(i):
            pos = i % POSITIONS
            return ring[:, 2 * pos:2 * pos + 2, :].rearrange("p s n -> p (s n)")

        def block_w(i, width, rows=KD):
            return at_block(i)[:, 0:rows * width].rearrange("p (k n) -> p k n", k=rows)

        def heads(ap):
            return ap.rearrange("p (h d) -> p h d", h=H)

        def logit_ps(tt, h):
            if tt == 0:
                return bank[4 + h % 2][:, (h // 2) * P:(h // 2 + 1) * P]
            return bank[(2 if h % 2 == 0 else 0) + h // 4][:, (h // 2 % 2) * T:(h // 2 % 2 + 1) * T]

        def prob(tt, h):
            return probs[:, h, KEY_AT[tt]:KEY_AT[tt] + KEYS[tt]]

        PROB_JOBS = [[(0, 4 * j + i, 0) for i in range(4)] for j in range(2)] + [
            [(1, 2 * j + i // 2, i % 2) for i in range(4)] for j in range(4)]
        PROB_AT = {u: BANK * j + P * i for j, job in enumerate(PROB_JOBS) for i, u in enumerate(job)}
        GATE_BANK = [2, 3, 4, 5]

        def w1_slot(parity, c):
            return ring[:, SLOT_W1[parity] + c, :]

        def w2_slot(c):
            return ring[:, SLOT_W2 + c, :]

        def w1_dram(e, c):
            return expert_w1[0][bass.ds(e, 1), c * P:(c + 1) * P, :].rearrange("a p n -> p (a n)")

        def w2_dram(e, c):
            return expert_w2[0][bass.ds(e, 1), c * 2 * P:(c + 1) * 2 * P, :].rearrange(
                "a (k p) n -> p (a k) n", p=P)

        PASSES = -(-(T - FIRST_SLOTS) // SLOTS)
        AHEAD = 3
        PASS_DMAS = W1_CHUNKS + W2_CHUNKS

        def gather(pe, tt):
            for half in range(2):
                mm = pe.matmul(ps_gather[SLOTS * half:SLOTS * (half + 1), :], pick[:, tt, :],
                               xn[:, tt, half * BANK:(half + 1) * BANK], start=(tt == 0), stop=(tt == TT - 1))
            return mm

        def gather_first(pe, tt):
            for k in range(KD):
                at = (k % 4) * P + (k // 4) * SLOTS
                mm = pe.matmul(ps_gather[:, at:at + SLOTS], xn[:, tt, k * P:(k + 1) * P], pick[:, tt, :],
                               start=(tt == 0 and k == 0), stop=(tt == TT - 1), skip_group_check=True)
            return mm

        def transpose_rows(pe):
            for j in range(4):
                mm = pe.transpose(ps_gather[:, j * P:(j + 1) * P], rows_e[:, j * P:(j + 1) * P], ident[:, :])
            return mm

        def transpose_put(pe):
            for tt in range(TT):
                mm = pe.transpose(ps_out[:, tt * P:(tt + 1) * P], put[:, tt, :], ident[:, :])
            return mm

        def up_bias(pe, first=True):
            for q in range(4):
                dst = (ps_gate, ps_lin)[q // 2][SLOTS * (q % 2):SLOTS * (q % 2 + 1), :]
                mm = pe.matmul(dst, bias_pick[:, q, :], b1_rows[:, :], start=first, stop=not first)
            return mm

        def up(pe, w, k, bias_first=True):
            at = (k % 4) * P + (k // 4) * SLOTS
            for q in range(4):
                dst = (ps_gate, ps_lin)[q // 2][SLOTS * (q % 2):SLOTS * (q % 2 + 1), :]
                mm = pe.matmul(dst, hTe[:, at:at + SLOTS], w[:, q * BANK:(q + 1) * BANK],
                               start=(k == 0 and not bias_first), stop=(k == KD - 1 and bias_first))
            return mm

        def transpose_act(pe):
            for j in range(4):
                mm = pe.transpose(ps_gate[:, j * P:(j + 1) * P], act_e[:, j * P:(j + 1) * P], ident[:, :])
            return mm

        def down(pe, w, c):
            for k in (2 * c, 2 * c + 1):
                at = (k % 4) * P + (k // 4) * SLOTS
                for half in range(2):
                    col = (k % 2) * D + half * BANK
                    mm = pe.matmul(ps_out[SLOTS * half:SLOTS * (half + 1), :], actT_e[:, at:at + SLOTS],
                                   w[:, col:col + BANK], start=(k == 0), stop=(k == 2 * W2_CHUNKS - 1))
            return mm

        def scatter(pe, rows, done=None):
            for tt in range(TT):
                for half in range(2):
                    mm = pe.matmul(acc[2 * tt + half][:, :], putT[rows, tt * P:(tt + 1) * P], out_pair[rows, half, :],
                                   start=False, stop=True, skip_group_check=True)
                    if done is not None:
                        mm.then_inc(done, 1)

        def build_pick(ids, e):
            for tt in range(TT):
                last = nc.vector.tensor_scalar(pick[:, tt, :], ids[:, 0:SLOTS], place[:, tt, bass.ds(e, 1)], None, ALU.is_equal)
            return last

        def build_put(ids, e):
            for tt in range(TT):
                last = nc.vector.tensor_scalar(put[:, tt, :], ids[:, :], place[:, tt, bass.ds(e, 1)],
                                               weight[:, tt, bass.ds(e, 1)], ALU.is_equal, ALU.mult)
            return last

        def build_bias_pick(e):
            one = ident[:, :].rearrange("p (q e) -> p q e", q=4)[:, :, bass.ds(e, 1)]
            return nc.vector.tensor_copy(bias_pick[:, :, :], one.to_broadcast([P, 4, SLOTS]))

        def rowsT_out():
            gain = vecs[:, V_G2:V_G2 + KD].rearrange("p (h j a) -> p j h a", h=2, a=1).to_broadcast([P, 4, 2, SLOTS])
            return nc.vector.tensor_tensor(hTe.rearrange("p (j h n) -> p j h n", j=4, h=2),
                                           ps_gather[:, :].rearrange("p (j h n) -> p j h n", j=4, h=2), gain, ALU.mult)

        def halves(parity):
            return slice(SLOTS * parity, SLOTS * (parity + 1))

        @block.sync
        def _(sp):
            for tt in range(TT):
                sp.dma_start(xs[:, tt, :], x[0, tt * P:(tt + 1) * P, :]).then_inc(x_in[tt], 16)

            def used(i):
                done, n = {B_IDX: (s["idx_ps"], 2), B_K: (s["k_ps"], TT), B_Q: (s["q_ps"], TT), B_V: (s["v_ps"], TT),
                           B_U: (s["uT_ps"], 2), B_WA: (s["branch_ps"], 2 * TT), B_WP: (s["branch_ps"], 2 * TT),
                           B_WO: (s["out_ps"], 2 * TT)}.get(i, (s["gate_ps"], TT * (i - B_G0 + 1)))
                sp.wait_ge(done, n)

            def load_block(i):
                if i == B_IDX:
                    dst, src = block_w(i, W_IDX), w_in[0][:, COL_IQ:COL_U]
                elif i < B_WA:
                    col = {B_K: DA, B_Q: 0, B_V: 2 * DA, B_U: COL_U}.get(i, COL_G + (i - B_G0) * BANK)
                    dst, src = block_w(i, BANK), w_in[0][:, col:col + BANK]
                elif i == B_WA:
                    dst, src = block_w(i, D, KA), w_branch_attn[0]
                elif i == B_WP:
                    dst, src = block_w(i, D, KA), w_branch_pool[0]
                else:
                    half = i - B_WO
                    dst, src = block_w(i, D, KD // 2), w_out[0][half * D // 2:(half + 1) * D // 2, :]
                if i >= POSITIONS:
                    used(i - POSITIONS)
                sp.dma_start(dst, src.rearrange("(k p) n -> p k n", p=P)).then_inc(block_in[i], 16)

            def load_w1(e, parity, c):
                sp.dma_start(w1_slot(parity, c), w1_dram(e, c)).then_inc(w1_in[parity][c], 16)

            def load_w2(e, c):
                sp.dma_start(w2_slot(c).rearrange("p (k n) -> p k n", k=2), w2_dram(e, c)).then_inc(w2_in[c], 16)

            for i in range(N_BLOCKS):
                load_block(i)
            used(B_G0 + 2)
            for c in (2, 3):
                load_w1(0, 0, c)
            sp.wait_ge(s["attn_ps"], TT)
            for c in (5, 6, 7):
                load_w1(1, 1, c)
            used(B_G0 + 3)
            for c in (4, 5):
                load_w1(0, 0, c)
            load_w1(1, 1, 0)
            used(B_WP)
            for c in (6, 7):
                load_w1(0, 0, c)
            for c in (0, 1):
                load_w2(0, c)
            load_w1(1, 1, 1)
            sp.wait_ge(s["mergedT_ps"], 2 * TT)
            for c in (2, 3, 4):
                load_w1(1, 1, c)
            used(B_WO)
            for c in (0, 1):
                load_w1(0, 0, c)
            for c in (2, 3):
                load_w2(0, c)

            def w1_of(e, parity):
                for c in range(W1_CHUNKS):
                    if c < W1_CHUNKS - 1:
                        sp.wait_ge(w1_used, e * (W1_CHUNKS - 1) + (c + 3 - 2 * W1_CHUNKS))
                    else:
                        sp.wait_ge(gemm1, e - 1)
                    load_w1(e, parity, c)

            def w2_of(e):
                for c in range(W2_CHUNKS):
                    if c < W2_CHUNKS - 1:
                        sp.wait_ge(w2_used, e * (W2_CHUNKS - 1) + (c + 2 - W2_CHUNKS))
                    else:
                        sp.wait_ge(gemm2, e)
                    load_w2(e, c)

            w1_of(2, 0)
            w2_of(1)
            with sp.Fori(0, AHEAD) as i:
                w1_of(2 * i + 3, 1)
                w2_of(2 * i + 2)
                w1_of(2 * i + 4, 0)
                w2_of(2 * i + 3)
            with sp.Fori(AHEAD, E // 2 - 2) as i:
                w2_of(2 * i + 2)
                w1_of(2 * i + 3, 1)
                w2_of(2 * i + 3)
                w1_of(2 * i + 4, 0)
            w2_of(E - 2)
            w1_of(E - 1, 1)
            w2_of(E - 1)

            sp.wait_ge(s["most_ok"], 1)
            most_reg = sp.value_load(most_i[0:1, 0:1], min_val=0, max_val=T)
            with sp.If(most_reg > FIRST_SLOTS):
                with sp.Fori(0, PASSES) as r:
                    with sp.Fori(0, E) as e:
                        sp.wait_ge(acc_done, (r * E + e) * (2 * TT) + 2 * TT)
                        for c in range(W1_CHUNKS):
                            sp.dma_start(w1_slot(0, c), w1_dram(e, c)).then_inc(f_w, 16)
                        for c in range(W2_CHUNKS):
                            sp.dma_start(w2_slot(c).rearrange("p (k n) -> p k n", k=2), w2_dram(e, c)).then_inc(f_w, 16)
            for j in range(2 * TT):
                tt, cols = j // 2, slice((j % 2) * BANK, (j % 2 + 1) * BANK)
                sp.wait_ge(s["result_ok"], j + 1)
                sp.dma_start(out[0, tt * P:(tt + 1) * P, cols], xs[:, tt, cols]).then_inc(s["stored"], 16)
            sp.wait_ge(s["stored"], 16 * 2 * TT)

        @block.gpsimd
        def _(pool):
            chain = Chain(pool, pool_step)
            chain.link(nc.gpsimd.memset(ident[:, :], 0.0))
            nc.gpsimd.affine_select(out=ident[:, :], in_=ident[:, :], compare_op=ALU.not_equal, fill=1.0,
                                    base=0, pattern=[[-1, P]], channel_multiplier=1).then_inc(s["ident_ok"], 1)
            chain.link(nc.gpsimd.memset(ones[:, :], 1.0))
            nc.gpsimd.affine_select(out=before[:, :], in_=ones[:, :], compare_op=ALU.is_gt, fill=0.0,
                                    base=0, pattern=[[1, P]], channel_multiplier=-1).then_inc(s["consts"], 1)
            nc.gpsimd.iota(slot_id[:, :], [[0, 2], [1, SLOTS]], base=1, channel_multiplier=0,
                           allow_small_or_imprecise_dtypes=True).then_inc(s["consts"], 1)
            nc.gpsimd.iota(expert_id[:, :], [[0, TOP_EXPERTS], [1, E]], base=0, channel_multiplier=0,
                           allow_small_or_imprecise_dtypes=True).then_inc(s["consts"], 1)
            chain.link(nc.gpsimd.iota(inv_count[:, :, :], [[0, G], [1, 16]], base=1, channel_multiplier=0,
                                      allow_small_or_imprecise_dtypes=True))
            for g, w in enumerate(POOL_WINDOWS):
                nc.gpsimd.tensor_scalar_min(inv_count[:, g, :], inv_count[:, g, :], float(w)).then_inc(s["consts"], 1)

            pool.wait_ge(s["uT_sb"], 2)
            pool.wait_ge(s["inv_ok"], 1)
            src = uT
            for j in range(G):
                dst = (sumT, diffT)[j % 2]
                sh, w = 1 << j, POOL_WINDOWS[j]
                nc.gpsimd.tensor_copy(dst[:, j:G, 0:sh], src[:, j:G, 0:sh]).then_inc(pool_step, 1)
                chain.n += 1
                chain.link(nc.gpsimd.tensor_tensor(dst[:, j:G, sh:T], src[:, j:G, sh:T], src[:, j:G, 0:T - sh], ALU.add))
                nc.gpsimd.tensor_tensor(diffT[:, j, 0:w], dst[:, j, 0:w], inv_count[:, j, 0:w], ALU.mult).then_inc(pool_step, 1)
                chain.n += 1
                chain.link(nc.gpsimd.tensor_scalar_mul(diffT[:, j, w:T], dst[:, j, w:T], 1.0 / w))
                nc.gpsimd.tensor_tensor(diffT[:, j, :], diffT[:, j, :], uT[:, j, :], ALU.subtract).then_inc(s["diff_ok"], 1)
                src = dst

        @block.scalar
        def _(act):
            chain = Chain(act, act_step)
            act.dma_start(gain_rows[:, :], attn_norm_g[0].rearrange("(k p) -> k p", p=P)).then_inc(s["gain_in"], 16)
            act.wait_ge(s["vec_ok"], 1)
            chain.link(nc.scalar.activation(stats[:, 0, 0:1], eps[:, 0:1], ACT.Sqrt))
            for tt in range(TT):
                act.wait_ge(x_in[tt], 16)
                chain.link(nc.scalar.activation(work[:, 1 + 2 * tt:3 + 2 * tt, :].rearrange("p a n -> p (a n)"), xs[:, tt, :],
                                                ACT.Square, accum_out=stats[:, 0, tt:tt + 1]))
                nc.scalar.activation(stats[:, 0, TT + tt:TT + tt + 1], stats[:, 0, tt:tt + 1], ACT.Sqrt,
                                     bias=eps[:, 0:1], scale=1.0 / D).then_inc(s["x_rms"], 1)
            act.wait_ge(s["vec_ok"], 2)
            for tt in range(TT):
                act.wait_ge(s["xT_ps"], 2 * tt + 2)
                for j in range(4):
                    k = 4 + j
                    nc.scalar.activation(hT[:, k, tt * P:(tt + 1) * P], bank[2 * tt + 1][:, j * P:(j + 1) * P], ACT.Copy,
                                         scale=vecs[:, V_G1 + k:V_G1 + k + 1]).then_inc(s["hT_act"], 1)
            for col, src, n in ((V_G2, ffn_norm_g, 8), (V_PB, pool_b, 4), (V_PS, pool_scale, 4)):
                row = col - V_G2
                act.dma_start(vec_rows[row:row + n, :], src[0].rearrange("(k p) -> k p", p=P)).then_inc(s["vec_row_ok"], 16)
            for row, src in ((V_QK - V_G2, q_norm_g), (V_QK + 1 - V_G2, k_norm_g)):
                act.dma_start(vec_rows[row:row + 1, :].rearrange("a (h d) -> a h d", h=2),
                              src.rearrange("a (h d) -> a h d", h=1).to_broadcast([1, 2, HD])).then_inc(s["vec_row_ok"], 16)
            act.dma_start(rw[:, :, :], router_w[0].rearrange("(k p) n -> p k n", p=P)).then_inc(small_in, 16)
            act.dma_start(rb[:, :], router_b.to_broadcast([P, E])).then_inc(small_in, 16)
            for q in range(4):
                act.dma_start(b1_rows[E * q:E * (q + 1), :], expert_b1[0][:, q * BANK:(q + 1) * BANK]).then_inc(small_in, 16)
            act.dma_start(pool_wsb[:, :, :], pool_w[0].rearrange("g c d -> c g d")).then_inc(small_in, 16)
            act.wait_ge(s["idx_ps"], 1)
            nc.scalar.copy(iqT[:, :, :], bank[4][:, :].rearrange("p (b t) -> p b t", b=2)).then_inc(s["idx_sb"], 1)
            act.wait_ge(s["idx_ps"], 2)
            nc.scalar.copy(iwT, bank[5][ID:ID + IH, 0:T]).then_inc(s["idx_sb"], 1)
            for r in range(2):
                nc.scalar.copy(ikT[ID * r:ID * (r + 1), :], bank[5][0:ID, 0:T]).then_inc(s["idx_sb"], 1)
            act.wait_ge(s["iw_ps"], 1)
            nc.scalar.mul(iw[:, :, :], bank[6][:, 0:TT * IH].rearrange("p (a h) -> p a h", a=TT), IH ** -0.5).then_inc(s["iw_sb"], 1)

            def square_heads(n, src):
                if n:
                    act.wait_ge(s["kq_ss"], n)
                nc.scalar.activation(squares, src, ACT.Square).then_inc(s["kq_sq"], 1)
                act.wait_ge(s["kq_ss"], n + 1)
                nc.scalar.activation(head_ss[:, n, :], head_ss[:, n, :], ACT.Sqrt, bias=eps[:, 0:1],
                                     scale=1.0 / HD).then_inc(s["kq_rms"], 1)

            for tt in range(TT):
                act.wait_ge(s["k_ps"], tt + 1)
                square_heads(tt, bank[tt][:, :])
            for tt in range(TT):
                act.wait_ge(s["dots_ps"], tt + 1)
                for r in range(2):
                    src = bank[2 + 2 * tt + r][:, 0:2 * KEYS[tt]].rearrange("p (b n) -> p b n", b=2)
                    dst = relu[:, r:IH:2, KEY_AT[tt]:KEY_AT[tt] + KEYS[tt]]
                    nc.scalar.activation(dst, src, ACT.Relu, scale=ID ** -0.5).then_inc(s["relu_ok"], 1)
            for tt in range(TT):
                act.wait_ge(s["q_ps"], tt + 1)
                square_heads(TT + tt, bank[6 + tt][:, :])
            for tt in range(TT):
                act.wait_ge(s["kT_ps"], tt + 1)
                nc.scalar.copy(kT[:, :, tt * P:(tt + 1) * P], bank[tt][:, :].rearrange("p (k t) -> p k t", k=KA)).then_inc(s["kT_sb"], 1)
            for tt in range(TT):
                act.wait_ge(s["v_ps"], tt + 1)
                nc.scalar.copy(v[:, tt, :], bank[2 + tt][:, :]).then_inc(s["v_sb"], 1)
            for b in range(2):
                act.wait_ge(s["uT_ps"], b + 1)
                nc.scalar.copy(uT[:, 2 * b:2 * b + 2, :], bank[6 + b][:, :].rearrange("p (g t) -> p g t", g=2)).then_inc(s["uT_sb"], 1)
            for tt in range(TT):
                act.wait_ge(s["negmax"], tt + 1)
                for h in range(H):
                    nc.scalar.activation(prob(tt, h), prob(tt, h), ACT.Exp, bias=neg_max[:, tt, h:h + 1],
                                         accum_out=den[:, tt, h:h + 1]).then_inc(s["prob_ok"], 1)

            def sigmoid(c, tt):
                n = TT * c + tt
                act.wait_ge(s["gate_ps"], n + 1)
                nc.scalar.activation(gates[:, tt, c * BANK:(c + 1) * BANK], bank[GATE_BANK[n % 4]][:, :],
                                     ACT.Sigmoid).then_inc(s["gate_sb"], 1)

            def probT_out(j):
                act.wait_ge(s["probT_ps"], j + 1)
                nc.scalar.copy(probsT[:, j * BANK:(j + 1) * BANK], bank[6 + j % 2][:, :]).then_inc(s["probT_sb"], 1)

            sigmoid(0, 0)
            sigmoid(0, 1)
            for c in (1, 2):
                for j in ((0, 1), (2, 3))[c - 1]:
                    probT_out(j)
                sigmoid(c, 0)
                for j in ((), (4, 5))[c - 1]:
                    probT_out(j)
                sigmoid(c, 1)
            sigmoid(3, 0)
            for b in range(2):
                act.wait_ge(s["pooled_ps"], b + 1)
                for g in (2 * b, 2 * b + 1):
                    chain.link(nc.scalar.activation(pooledT[:, g, :], bank[b][:, (g % 2) * T:(g % 2 + 1) * T], ACT.Identity,
                                                    bias=vecs[:, V_PB + g:V_PB + g + 1]))
                    nc.scalar.activation(pooledT[:, g, :], pooledT[:, g, :], ACT.Copy,
                                         scale=vecs[:, V_PS + g:V_PS + g + 1]).then_inc(s["pooled_sb"], 1)
            sigmoid(3, 1)
            for j in range(2 * TT):
                act.wait_ge(s["mergedT_ps"], j + 1)
                tt, half = j // 2, j % 2
                nc.scalar.copy(mergedT[tt][:, 4 * half:4 * half + 4, :],
                               bank[6 + half][:, :].rearrange("p (k t) -> p k t", k=4)).then_inc(s["mergedT_sb"], 1)
            act.wait_ge(s["attn_ps"], TT)
            act.dma_start(b2_all, expert_b2[0]).then_inc(b2_in, 16)
            for tt in range(TT):
                part = stats[:, 1, 2 * tt:2 * tt + 1]
                rms = stats[:, 1, 2 * tt + 1:2 * tt + 2]
                act.wait_ge(s["x1_ok"], 2 * tt + 1)
                chain.link(nc.scalar.activation(hTe, xs[:, tt, 0:BANK], ACT.Square, accum_out=part))
                chain.link(nc.scalar.activation(part, part, ACT.Identity, bias=eps[:, 0:1], scale=1.0 / D))
                for b in range(2 - tt):
                    act.wait_ge(s["x1T_ps"], 2 * tt + b + 1)
                    nc.scalar.copy(x1T[:, 2 * tt + b, :, :], bank[4 + 2 * tt + b][:, :].rearrange("p (k t) -> p k t", k=4)).then_inc(s["x1T_act"], 1)
                act.wait_ge(s["x1_ok"], 2 * tt + 2)
                chain.link(nc.scalar.activation(hTe, xs[:, tt, BANK:D], ACT.Square, accum_out=rms))
                nc.scalar.activation(rms, rms, ACT.Sqrt, bias=part, scale=1.0 / D).then_inc(s["x1_rms"], 1)
                if tt:
                    act.wait_ge(s["weightT_ps"], 1)
                    nc.scalar.copy(weightT[:, 0:P], ps_lin[0:E, 0:P]).then_inc(s["weightT_sb"], 1)
                act.wait_ge(s["rt_top"], tt + 1)
                nc.scalar.activation(rexp[:, tt, 0:TOP_EXPERTS], rt8[:, tt, 0:TOP_EXPERTS], ACT.Exp,
                                     bias=rsum[:, tt, 0:1], accum_out=rsum[:, tt, 1:2]).then_inc(s["rt_exp"], 1)
                if tt == 0:
                    nc.scalar.activation(stats[:, 0, 0:1], eps[:, 0:1], ACT.Sqrt).then_inc(act_step, 1)
                    chain.n += 1
            act.wait_ge(s["weightT_ps"], 2)
            nc.scalar.copy(weightT[:, P:T], acc[3][0:E, P:T]).then_inc(s["weightT_sb"], 1)

            def expert(e, parity, last=False):
                act.wait_ge(gate_ok, e + 1)
                nc.scalar.activation(sig_e, gate_e, ACT.Sigmoid, scale=SWIGLU_ALPHA).then_inc(sig_ok, 1)
                act.wait_ge(put_ps, e + 1)
                nc.scalar.copy(putT[halves(parity), :], ps_out[halves(parity), 0:T]).then_inc(put_sb, 1)
                if not last:
                    act.wait_ge(gathered, e + 1)
                    act.wait_ge(glu_ok, e + 1)
                    nc.scalar.copy(rows_e, ps_gather[:, :]).then_inc(rows_ok, 1)
                act.wait_ge(actT_ps, e + 1)
                nc.scalar.copy(actT_e, ps_gate[:, :]).then_inc(actT_sb, 1)
                act.wait_ge(gemm2, e + 1)
                nc.scalar.copy(out_pair[halves(parity), 0, :], ps_out[0:SLOTS, :]).then_inc(out_ok, 1)

            with act.Fori(0, E // 2 - 1) as i:
                expert(2 * i, 0)
                expert(2 * i + 1, 1)
            expert(E - 2, 0)
            expert(E - 1, 1, last=True)

            act.wait_ge(s["most_ok"], 1)
            most_reg = act.value_load(most_i[0:1, 0:1], min_val=0, max_val=T)
            with act.If(most_reg > FIRST_SLOTS):
                with act.Fori(0, PASSES * E) as n:
                    act.wait_ge(f_ps, n + 1)
                    nc.scalar.copy(putT[halves(0), :], ps_out[halves(0), 0:T])
                    nc.scalar.copy(rows_e, ps_gather[:, :]).then_inc(f_rows, 1)
                    act.wait_ge(f_gate, n + 1)
                    nc.scalar.activation(sig_e, gate_e, ACT.Sigmoid, scale=SWIGLU_ALPHA).then_inc(f_sig, 1)
                    act.wait_ge(f_actT, n + 1)
                    nc.scalar.copy(actT_e, ps_gate[:, :]).then_inc(f_actTs, 1)
                    act.wait_ge(f_g2, n + 1)
                    for half in range(2):
                        nc.scalar.copy(out_pair[halves(0), half, :], ps_out[halves(half), :]).then_inc(f_out, 1)

        @block.vector
        def _(dve):
            chain = Chain(dve, dve_step)
            nc.vector.memset(eps[:, :], EPS).then_inc(s["vec_ok"], 1)
            dve.wait_ge(s["vec_ps"], 1)
            nc.vector.tensor_copy(vecs[:, V_G1:V_G2], ps_out[:, V_G1:V_G2]).then_inc(s["vec_ok"], 1)
            for tt in range(TT):
                dve.wait_ge(s["x_rms"], tt + 1)
                chain.link(nc.vector.reciprocal(stats[:, 0, TT + tt:TT + tt + 1], stats[:, 0, TT + tt:TT + tt + 1]))
                nc.vector.tensor_scalar(xn[:, tt, :], xs[:, tt, :], stats[:, 0, TT + tt:TT + tt + 1], None, ALU.mult).then_inc(s["x_norm"], 1)
            dve.wait_ge(s["vec_ok"], 2)
            for tt in range(TT):
                dve.wait_ge(s["xT_ps"], 2 * tt + 1)
                gain = vecs[:, V_G1:V_G1 + 4].rearrange("p (k a) -> p k a", a=1).to_broadcast([P, 4, P])
                nc.vector.tensor_tensor(hT[:, 0:4, tt * P:(tt + 1) * P], bank[2 * tt][:, :].rearrange("p (k t) -> p k t", k=4),
                                        gain, ALU.mult).then_inc(s["hT_dve"], 1)
            dve.wait_ge(s["consts"], 3 + G)
            nc.vector.reciprocal(inv_count[:, :, :], inv_count[:, :, :]).then_inc(s["inv_ok"], 1)

            def norm_heads(n, src, dst):
                dve.wait_ge(s["kq_sq"], n + 1)
                nc.vector.tensor_reduce(head_ss[:, n, :], heads(squares), AX_X, ALU.add).then_inc(s["kq_ss"], 1)
                dve.wait_ge(s["kq_rms"], n + 1)
                chain.link(nc.vector.reciprocal(head_ss[:, n, :], head_ss[:, n, :]))
                inv = head_ss[:, n, :].rearrange("p (h a) -> p h a", a=1).to_broadcast([P, H, HD])
                nc.vector.tensor_tensor(heads(dst), heads(src), inv, ALU.mult).then_inc(s["kq_norm"], 1)

            for tt in range(TT):
                norm_heads(tt, bank[tt][:, :], kn[:, tt, :])
            dve.wait_ge(s["iw_sb"], 1)
            for tt in range(TT):
                keys = slice(KEY_AT[tt], KEY_AT[tt] + KEYS[tt])
                dve.wait_ge(s["relu_ok"], 2 * tt + 2)
                chain.link(nc.vector.tensor_scalar(score[:, keys], relu[:, 0, keys], iw[:, tt, 0:1], None, ALU.mult))
                for h in range(1, IH):
                    chain.link(nc.vector.scalar_tensor_tensor(out=score[:, keys], in0=relu[:, h, keys], scalar=iw[:, tt, h:h + 1],
                                                              in1=score[:, keys], op0=ALU.mult, op1=ALU.add))
                chain.link(nc.vector.memset(score[0:CHUNK, keys.stop - CHUNK:keys.stop], INADMISSIBLE))
                for _ in range(TOPK // 8):
                    chain.link(nc.vector.max(top8[:, tt, :], score[:, keys]))
                    chain.link(nc.vector.match_replace(out=score[:, keys], in_to_replace=top8[:, tt, :],
                                                       in_values=score[:, keys], imm_value=TAKEN))
            nc.vector.tensor_scalar(unselected, score, (TAKEN + INADMISSIBLE) / 2, NOT_SELECTED,
                                    ALU.is_gt, ALU.mult).then_inc(s["mask_ok"], 1)
            for tt in range(TT):
                norm_heads(TT + tt, bank[6 + tt][:, :], qn[:, tt, :])
            dve.wait_ge(s["vec_ps"], 2)
            nc.vector.tensor_copy(vecs[:, V_G2:26], bank[4][:, 0:18]).then_inc(s["vec_ok"], 1)
            dve.wait_ge(s["vec_ok"], 3)
            chain.link(nc.vector.tensor_tensor(qk_gain[:, :], vecs[:, V_QK:V_QK + 1], vecs[:, V_QK + 1:V_QK + 2], ALU.mult))
            chain.link(nc.vector.tensor_scalar(qk_gain[:, :], qk_gain[:, :], HD ** -0.5, None, ALU.mult))
            for tt in range(TT):
                dve.wait_ge(s["qT_ps"], tt + 1)
                nc.vector.tensor_scalar(qT[:, :, tt * P:(tt + 1) * P], bank[6 + tt][:, :].rearrange("p (k t) -> p k t", k=KA),
                                        qk_gain[:, 0:1], None, ALU.mult).then_inc(s["qT_sb"], 1)
            dve.wait_ge(s["mask_ok"], 1)
            for tt in range(TT):
                dve.wait_ge(s["logit_ps"], tt + 1)
                for h in range(H):
                    nc.vector.tensor_tensor_reduce(
                        out=prob(tt, h), in0=logit_ps(tt, h), in1=unselected[:, KEY_AT[tt]:KEY_AT[tt] + KEYS[tt]],
                        scale=1.0, scalar=TAKEN, op0=ALU.add, op1=ALU.max, accum_out=max_l[:, tt, h:h + 1]).then_inc(s["masked"], 1)
                dve.wait_ge(s["masked"], H * (tt + 1))
                nc.vector.tensor_scalar(neg_max[:, tt, :], max_l[:, tt, :], -1.0, None, ALU.mult).then_inc(s["negmax"], 1)
            dve.wait_ge(small_in, 16 * 7)
            gain = vecs[:, V_G2:V_G2 + KD].rearrange("p (k a) -> p k a", a=1).to_broadcast([P, KD, E])
            nc.vector.tensor_tensor(rw[:, :, :], rw[:, :, :], gain, ALU.mult).then_inc(s["rw_ok"], 1)
            for tt in range(TT):
                dve.wait_ge(s["prob_ok"], H * (tt + 1))
                chain.link(nc.vector.reciprocal(den[:, tt, :], den[:, tt, :]))
                dve.wait_ge(s["attn_ps"], tt + 1)
                inv = den[:, tt, :].rearrange("p (h a) -> p h a", a=1).to_broadcast([P, H, HD])
                nc.vector.tensor_tensor(heads(attn[:, tt, :]), heads(bank[tt][:, :]), inv, ALU.mult).then_inc(s["attn_ok"], 1)
            for tt in range(TT):
                dve.wait_ge(s["attnT_ps"], tt + 1)
                nc.vector.tensor_copy(attnT[:, :, tt * P:(tt + 1) * P], bank[6 + tt][:, :].rearrange("p (k t) -> p k t", k=KA)).then_inc(s["attnT_sb"], 1)
            dve.wait_ge(s["gate_sb"], 4 * TT)
            for j in range(2 * TT):
                tt, half = j // 2, j % 2
                cols = slice(half * BANK, (half + 1) * BANK)
                g_p = gates[:, tt, D + half * BANK:D + (half + 1) * BANK]
                dve.wait_ge(s["branch_ps"], j + 1)
                nc.vector.tensor_tensor(merged[:, tt, cols], bank[2 + 2 * (j % 2)][:, :], gates[:, tt, cols], ALU.mult).then_inc(dve_step, 1)
                chain.n += 1
                chain.link(nc.vector.tensor_tensor(g_p, bank[3 + 2 * (j % 2)][:, :], g_p, ALU.mult))
                nc.vector.tensor_tensor(merged[:, tt, cols], merged[:, tt, cols], g_p, ALU.add).then_inc(s["merge_ok"], 1)
            def add_out(j):
                tt, half = j // 2, j % 2
                cols = slice(half * BANK, (half + 1) * BANK)
                dve.wait_ge(s["out_ps"], j + 1)
                nc.vector.tensor_tensor(xs[:, tt, cols], xs[:, tt, cols], bank[j][:, :], ALU.add).then_inc(s["x1_ok"], 1)

            hot = onehot[:, 0, :].rearrange("p (k e) -> p k e", k=TOP_EXPERTS)
            weighted = onehot[:, 1, :].rearrange("p (k e) -> p k e", k=TOP_EXPERTS)

            def choose(tt):
                rstd = stats[:, 1, 2 * tt + 1:2 * tt + 2]
                dve.wait_ge(s["x1_rms"], tt + 1)
                chain.link(nc.vector.reciprocal(rstd, rstd))
                dve.wait_ge(s["logits2_ps"], tt + 1)
                nc.vector.scalar_tensor_tensor(out=logit[:, tt, :], in0=bank[7 - tt][:, 0:E],
                                               scalar=rstd, in1=rb[:, :], op0=ALU.mult, op1=ALU.add).then_inc(s["logits2_read"], 1)
                dve.wait_ge(s["logits2_read"], tt + 1)
                chain.link(nc.vector.max(rt8[:, tt, :], logit[:, tt, :]))
                chain.link(nc.vector.max_index(out=ri8[:, tt, :], in_max=rt8[:, tt, :], in_values=logit[:, tt, :]))
                chain.link(nc.vector.tensor_copy(rid[:, tt, :], ri8[:, tt, :]))
                ids = rid[:, tt, 0:TOP_EXPERTS].rearrange("p (k a) -> p k a", a=1).to_broadcast([P, TOP_EXPERTS, E])
                chain.link(nc.vector.tensor_tensor(hot, expert_id[:, :].rearrange("p (k e) -> p k e", k=TOP_EXPERTS), ids, ALU.is_equal))
                nc.vector.tensor_reduce(chosen[:, tt, :], onehot[:, 0, :].rearrange("p (k e) -> p e k", k=TOP_EXPERTS), AX_X, ALU.add).then_inc(s["rt_ok"], 1)
                nc.vector.tensor_scalar(rsum[:, tt, 0:1], rt8[:, tt, 0:1], -1.0, None, ALU.mult).then_inc(s["rt_top"], 1)
                nc.vector.tensor_scalar(xn[:, tt, :], xs[:, tt, :], rstd, None, ALU.mult)

            def weigh(tt):
                dve.wait_ge(s["rt_exp"], tt + 1)
                chain.link(nc.vector.reciprocal(rsum[:, tt, 2:3], rsum[:, tt, 1:2]))
                share = rexp[:, tt, 0:TOP_EXPERTS].rearrange("p (k a) -> p k a", a=1).to_broadcast([P, TOP_EXPERTS, E])
                chain.link(nc.vector.scalar_tensor_tensor(out=weighted, in0=hot, scalar=rsum[:, tt, 2:3], in1=share, op0=ALU.mult, op1=ALU.mult))
                nc.vector.tensor_reduce(weight[:, tt, :], onehot[:, 1, :].rearrange("p (k e) -> p e k", k=TOP_EXPERTS), AX_X, ALU.add).then_inc(s["weight_ok"], 1)

            def locate(tt):
                dve.wait_ge(s["place_ps"], tt + 1)
                nc.vector.scalar_tensor_tensor(out=place[:, tt, :], in0=ps_gate[:, tt * E:(tt + 1) * E], scalar=1.0,
                                               in1=chosen[:, tt, :], op0=ALU.add, op1=ALU.mult).then_inc(s["place_ok"], 1)
                dve.wait_ge(s["place_ok"], tt + 1)
                nc.vector.tensor_scalar(pick[:, tt, :], slot_id[:, 0:SLOTS], place[:, tt, 0:1], None, ALU.is_equal).then_inc(s["first_pick"], 1)

            for j in range(3):
                add_out(j)
            choose(0)
            weigh(0)
            add_out(3)
            dve.wait_ge(s["x1T_ps"], 2 * TT)
            nc.vector.tensor_copy(x1T[:, 3, :, :], bank[7][:, :].rearrange("p (k t) -> p k t", k=4)).then_inc(s["x1T_dve"], 1)
            locate(0)
            choose(1)
            locate(1)
            chain.link(nc.vector.tensor_reduce(most[0:1, 0:1], ps_gate[0:1, 2 * E:3 * E], AX_X, ALU.max))
            nc.vector.tensor_copy(most_i[0:1, 0:1], most[0:1, 0:1]).then_inc(s["most_ok"], 1)
            build_bias_pick(0).then_inc(s["bias_ok"], 1)
            weigh(1)
            nc.vector.tensor_scalar(slot_fb[:, :], slot_id[:, :], float(FIRST_SLOTS - SLOTS), None, ALU.add).then_inc(f_ids, 1)

            def following(e, more=True):
                dve.wait_ge(rowsT_ps, e + 1)
                rowsT_out().then_inc(hTe_ok, 1)
                if more:
                    build_pick(slot_id, e + 1).then_inc(pick_ok, 1)

            def expert(e, parity, more=True, more2=True):
                dve.wait_ge(gemm1, e + 1)
                nc.vector.tensor_scalar(gate_e, ps_gate[:, :], SWIGLU_LIMIT, None, ALU.min).then_inc(gate_ok, 1)
                nc.vector.tensor_scalar(lin_e, ps_lin[:, :], SWIGLU_LIMIT, -SWIGLU_LIMIT, ALU.min, ALU.max).then_inc(lin_ok, 1)
                dve.wait_ge(gate_ok, e + 1)
                dve.wait_ge(lin_ok, e + 1)
                nc.vector.scalar_tensor_tensor(out=lin_e, in0=lin_e, scalar=1.0, in1=gate_e, op0=ALU.add,
                                               op1=ALU.mult).then_inc(half_ok, 1)
                dve.wait_ge(half_ok, e + 1)
                dve.wait_ge(sig_ok, e + 1)
                nc.vector.tensor_tensor(act_e, lin_e, sig_e, ALU.mult).then_inc(glu_ok, 1)
                if more:
                    build_bias_pick(e + 1).then_inc(s["bias_ok"], 1)
                    following(e + 1, more2)
                    dve.wait_ge(put_ps, e + 1)
                    build_put(slot_id, e + 1).then_inc(put_ok, 1)
                dve.wait_ge(gemm2, e + 1)
                nc.vector.tensor_copy(out_pair[halves(parity), 1, :], ps_out[SLOTS:P, :]).then_inc(out2_ok, 1)

            following(0)
            dve.wait_ge(s["weight_ok"], TT)
            build_put(slot_id, 0).then_inc(put_ok, 1)
            expert(0, 0)
            with dve.Fori(0, E // 2 - 2) as i:
                expert(2 * i + 1, 1)
                expert(2 * i + 2, 0)
            expert(E - 3, 1)
            expert(E - 2, 0, more2=False)
            expert(E - 1, 1, more=False)

            most_reg = dve.value_load(most_i[0:1, 0:1], min_val=0, max_val=T)
            with dve.If(most_reg > FIRST_SLOTS):
                with dve.Fori(0, PASSES) as r:
                    dve.wait_ge(acc_done, r * (2 * TT * E) + 2 * TT)
                    nc.vector.tensor_scalar(slot_fb[:, :], slot_fb[:, :], float(SLOTS), None, ALU.add).then_inc(f_ids, 1)
                    with dve.Fori(0, E) as e:
                        n = r * E + e
                        dve.wait_ge(f_ids, r + 2)
                        dve.wait_ge(acc_done, n * (2 * TT) + 2 * TT)
                        build_bias_pick(e)
                        build_pick(slot_fb, e)
                        build_put(slot_fb, e).then_inc(f_pick, 1)
                        dve.wait_ge(f_rowsT, n + 1)
                        rowsT_out().then_inc(f_hT, 1)
                        dve.wait_ge(f_g1, n + 1)
                        nc.vector.tensor_scalar(gate_e, ps_gate[:, :], SWIGLU_LIMIT, None, ALU.min).then_inc(f_gate, 1)
                        nc.vector.tensor_scalar(lin_e, ps_lin[:, :], SWIGLU_LIMIT, -SWIGLU_LIMIT, ALU.min, ALU.max).then_inc(f_lin, 1)
                        dve.wait_ge(f_gate, n + 1)
                        dve.wait_ge(f_lin, n + 1)
                        nc.vector.scalar_tensor_tensor(out=lin_e, in0=lin_e, scalar=1.0, in1=gate_e, op0=ALU.add,
                                                       op1=ALU.mult).then_inc(f_half, 1)
                        dve.wait_ge(f_half, n + 1)
                        dve.wait_ge(f_sig, n + 1)
                        nc.vector.tensor_tensor(act_e, lin_e, sig_e, ALU.mult).then_inc(f_glu, 1)
                dve.wait_ge(acc_done, 2 * TT * (PASSES * E + 1))
            for j in range(2 * TT):
                tt, half = j // 2, j % 2
                cols = slice(half * BANK, (half + 1) * BANK)
                dve.wait_ge(acc_done, j + 1)
                nc.vector.tensor_tensor(xs[:, tt, cols], xs[:, tt, cols], acc[j][:, :], ALU.add).then_inc(s["result_ok"], 1)

        @block.tensor
        def _(pe):
            pe.wait_ge(s["ident_ok"], 1)
            pe.wait_ge(s["gain_in"], 16)
            pe.transpose(ps_out[:, V_G1:V_G2], gain_rows[:, :], ident[0:8, 0:8]).then_inc(s["vec_ps"], 1)
            for tt in range(TT):
                pe.wait_ge(s["x_norm"], tt + 1)
                for b in range(2):
                    for j in range(4):
                        mm = pe.transpose(bank[2 * tt + b][:, j * P:(j + 1) * P], xn[:, tt, (4 * b + j) * P:(4 * b + j + 1) * P], ident[:, :])
                    mm.then_inc(s["xT_ps"], 1)
            pe.wait_ge(s["hT_dve"], TT)
            pe.wait_ge(s["hT_act"], 4 * TT)
            pe.wait_ge(s["vec_ok"], 2)

            pe.wait_ge(block_in[B_IDX], 16)
            w = block_w(B_IDX, W_IDX)
            for b in range(2):
                for k in range(KD):
                    mm = pe.matmul(bank[4][:, b * T:(b + 1) * T], w[:, k, b * P:(b + 1) * P], hT[:, k, :], start=(k == 0), stop=(k == KD - 1))
            mm.then_inc(s["idx_ps"], 1)
            for k in range(KD):
                mm = pe.matmul(bank[5][0:ID + IH, 0:T], w[:, k, IH * ID:W_IDX], hT[:, k, :], start=(k == 0), stop=(k == KD - 1))
            mm.then_inc(s["idx_ps"], 1)

            def project(i, tt, dst, done):
                w = block_w(i, BANK)
                for k in range(KD):
                    mm = pe.matmul(dst, hT[:, k, tt * P:(tt + 1) * P], w[:, k, :], start=(k == 0), stop=(k == KD - 1))
                mm.then_inc(done, 1)

            pe.wait_ge(block_in[B_K], 16)
            project(B_K, 0, bank[0][:, :], s["k_ps"])
            pe.wait_ge(s["idx_sb"], 2)
            for tt in range(TT):
                mm = pe.transpose(bank[6][:, tt * IH:(tt + 1) * IH], iwT[:, tt * P:(tt + 1) * P], ident[0:IH, 0:IH])
            mm.then_inc(s["iw_ps"], 1)
            project(B_K, 1, bank[1][:, :], s["k_ps"])
            pe.wait_ge(s["idx_sb"], 4)
            for tt in range(TT):
                for b in range(2):
                    for r in range(2):
                        rows = slice(ID * r, ID * (r + 1))
                        mm = pe.matmul(bank[2 + 2 * tt + r][:, b * KEYS[tt]:(b + 1) * KEYS[tt]], iqT[rows, b, tt * P:(tt + 1) * P],
                                       ikT[rows, 0:KEYS[tt]], start=True, stop=True)
                mm.then_inc(s["dots_ps"], 1)
            pe.wait_ge(s["iw_sb"], 1)
            pe.wait_ge(block_in[B_Q], 16)
            for tt in range(TT):
                project(B_Q, tt, bank[6 + tt][:, :], s["q_ps"])
            pe.wait_ge(block_in[B_V], 16)
            pe.wait_ge(s["relu_ok"], 4)

            def transpose_kq(n):
                src, dst, done = (kn, bank[n], s["kT_ps"]) if n < TT else (qn, bank[4 + n], s["qT_ps"])
                pe.wait_ge(s["kq_norm"], n + 1)
                for j in range(KA):
                    mm = pe.transpose(dst[:, j * P:(j + 1) * P], src[:, n % TT, j * P:(j + 1) * P], ident[:, :])
                mm.then_inc(done, 1)

            transpose_kq(0)
            transpose_kq(1)
            pe.wait_ge(s["vec_row_ok"], 16 * 5)
            pe.transpose(bank[4][:, 0:18], vec_rows[:, :], ident[0:18, 0:18]).then_inc(s["vec_ps"], 1)
            project(B_V, 0, bank[2][:, :], s["v_ps"])
            transpose_kq(2)
            transpose_kq(3)
            project(B_V, 1, bank[3][:, :], s["v_ps"])
            pe.wait_ge(s["kT_sb"], TT)
            pe.wait_ge(s["qT_sb"], TT)
            for tt in range(TT):
                if tt:
                    pe.wait_ge(s["v_sb"], TT)
                for h in range(H):
                    rows = slice(HD * (h % 2), HD * (h % 2 + 1))
                    mm = pe.matmul(logit_ps(tt, h), qT[rows, h // 2, tt * P:(tt + 1) * P], kT[rows, h // 2, 0:KEYS[tt]],
                                   start=True, stop=True)
                mm.then_inc(s["logit_ps"], 1)
            pe.wait_ge(block_in[B_U], 16)
            w = block_w(B_U, BANK)
            for g in range(G):
                for k in range(KD):
                    mm = pe.matmul(bank[6 + g // 2][:, (g % 2) * T:(g % 2 + 1) * T], w[:, k, g * P:(g + 1) * P], hT[:, k, :],
                                   start=(k == 0), stop=(k == KD - 1))
                if g % 2:
                    mm.then_inc(s["uT_ps"], 1)

            def gate(c, tt):
                n = TT * c + tt
                if tt == 0:
                    pe.wait_ge(block_in[B_G0 + c], 16)
                if n >= 4:
                    pe.wait_ge(s["gate_sb"], n - 3)
                project(B_G0 + c, tt, bank[GATE_BANK[n % 4]][:, :], s["gate_ps"])

            def transpose_probs(j):
                for i, (tt, h, kb) in enumerate(PROB_JOBS[j]):
                    mm = pe.transpose(bank[6 + j % 2][:, i * P:(i + 1) * P], prob(tt, h)[:, kb * P:(kb + 1) * P], ident[:, :])
                mm.then_inc(s["probT_ps"], 1)

            def attend(tt):
                for h in range(H):
                    for kb in range(tt + 1):
                        at = PROB_AT[(tt, h, kb)]
                        mm = pe.matmul(bank[tt][:, h * HD:(h + 1) * HD], probsT[:, at:at + P], v[:, kb, h * HD:(h + 1) * HD],
                                       start=(kb == 0), stop=(kb == tt))
                mm.then_inc(s["attn_ps"], 1)

            pe.wait_ge(s["masked"], 2 * H)
            gate(0, 0)
            gate(0, 1)
            pe.wait_ge(s["uT_sb"], 2)
            pe.wait_ge(s["prob_ok"], H)
            transpose_probs(0)
            transpose_probs(1)
            gate(1, 0)
            pe.wait_ge(s["probT_sb"], 2)
            attend(0)
            gate(1, 1)
            pe.wait_ge(s["prob_ok"], 2 * H)
            transpose_probs(2)
            transpose_probs(3)
            gate(2, 0)
            for j in (4, 5):
                pe.wait_ge(s["probT_sb"], j - 1)
                transpose_probs(j)
            gate(2, 1)
            pe.wait_ge(s["probT_sb"], 6)
            attend(1)
            gate(3, 0)
            for tt in range(TT):
                pe.wait_ge(s["attn_ok"], tt + 1)
                for j in range(KA):
                    mm = pe.transpose(bank[6 + tt][:, j * P:(j + 1) * P], attn[:, tt, j * P:(j + 1) * P], ident[:, :])
                mm.then_inc(s["attnT_ps"], 1)
            pe.wait_ge(small_in, 16 * 7)
            pe.wait_ge(s["diff_ok"], G)
            for g in range(G):
                mm = pe.matmul(bank[g // 2][:, (g % 2) * T:(g % 2 + 1) * T], pool_wsb[:, g, :], diffT[:, g, :], start=True, stop=True)
                if g % 2:
                    mm.then_inc(s["pooled_ps"], 1)
            gate(3, 1)
            for i in (B_WA, B_WP):
                pe.wait_ge(block_in[i], 16)
            pe.wait_ge(s["attnT_sb"], TT)
            pe.wait_ge(s["pooled_sb"], G)

            def branches(j):
                tt, half = j // 2, j % 2
                if j >= 2:
                    pe.wait_ge(s["merge_ok"], j - 1)
                else:
                    pe.wait_ge(s["gate_sb"], 2 * (j + 3))
                for n, (src, i) in enumerate(((attnT, B_WA), (pooledT, B_WP))):
                    w = block_w(i, D, KA)
                    for k in range(KA):
                        mm = pe.matmul(bank[2 + 2 * (j % 2) + n][:, :], src[:, k, tt * P:(tt + 1) * P],
                                       w[:, k, half * BANK:(half + 1) * BANK], start=(k == 0), stop=(k == KA - 1))
                mm.then_inc(s["branch_ps"], 1)

            def transpose_merged(tt):
                for half in range(2):
                    pe.wait_ge(s["merge_ok"], 2 * tt + half + 1)
                    if tt:
                        pe.wait_ge(s["mergedT_sb"], half + 1)
                    else:
                        pe.wait_ge(s["attnT_sb"], TT)
                    for j in range(4):
                        mm = pe.transpose(bank[6 + half][:, j * P:(j + 1) * P], merged[:, tt, (4 * half + j) * P:(4 * half + j + 1) * P], ident[:, :])
                    mm.then_inc(s["mergedT_ps"], 1)

            def project_out(tt, half, blocks=range(KD)):
                pe.wait_ge(s["mergedT_sb"], 2 * tt + 2)
                for k in blocks:
                    w = block_w(B_WO + k // 4, D, KD // 2)
                    mm = pe.matmul(bank[2 * tt + half][:, :], mergedT[tt][:, k, :],
                                   w[:, k % 4, half * BANK:(half + 1) * BANK], start=(k == 0), stop=(k == KD - 1))
                if k == KD - 1:
                    mm.then_inc(s["out_ps"], 1)

            def transpose_x1(tt, b):
                pe.wait_ge(s["x1_ok"], 2 * tt + b + 1)
                for j in range(4):
                    mm = pe.transpose(bank[4 + 2 * tt + b][:, j * P:(j + 1) * P], xs[:, tt, (4 * b + j) * P:(4 * b + j + 1) * P], ident[:, :])
                mm.then_inc(s["x1T_ps"], 1)

            def route(tt):
                for k in range(KD):
                    if k == 0:
                        pe.wait_ge(s["x1T_act"], 2 + tt)
                    if tt and k == KD // 2:
                        pe.wait_ge(s["x1T_dve"], 1)
                    mm = pe.matmul(bank[7 - tt][:, 0:E], x1T[:, 2 * tt + k // 4, k % 4, :], rw[:, k, :], start=(k == 0), stop=(k == KD - 1))
                mm.then_inc(s["logits2_ps"], 1)

            def place_tokens(tt):
                pe.wait_ge(s["rt_ok"], tt + 1)
                for at, w in (((0, before), (E, ones), (2 * E, ones)), ((E, before), (2 * E, ones)))[tt]:
                    mm = pe.matmul(ps_gate[:, at:at + E], w[:, :], chosen[:, tt, :], start=(tt == 0 and at == 0),
                                   stop=True, skip_group_check=True)
                mm.then_inc(s["place_ps"], 1)

            def transpose_weight(tt):
                pe.wait_ge(s["weight_ok"], tt + 1)
                pe.transpose((acc[3] if tt else ps_lin)[0:E, tt * P:(tt + 1) * P], weight[:, tt, :], ident[:, :]).then_inc(s["weightT_ps"], 1)

            def start_acc(j):
                return pe.matmul(acc[j][:, :], weightT[:, (j // 2) * P:(j // 2 + 1) * P], b2_all[:, (j % 2) * BANK:(j % 2 + 1) * BANK],
                                 start=True, stop=True, skip_group_check=True)

            for j in range(3):
                branches(j)
            transpose_merged(0)
            branches(3)
            for i in (B_WO, B_WO + 1):
                pe.wait_ge(block_in[i], 16)
            pe.wait_ge(s["pooled_sb"], G)
            project_out(0, 0)
            transpose_merged(1)
            project_out(0, 1)
            pe.wait_ge(s["merge_ok"], 2 * TT)
            project_out(1, 0)
            transpose_x1(0, 0)
            transpose_x1(0, 1)
            pe.wait_ge(s["rw_ok"], 1)
            project_out(1, 1, range(0, 2))
            route(0)
            project_out(1, 1, range(2, 6))
            pe.wait_ge(s["consts"], 3 + G)
            place_tokens(0)
            transpose_weight(0)
            project_out(1, 1, range(6, KD))
            transpose_x1(1, 0)
            pe.wait_ge(s["logits2_read"], 1)
            transpose_x1(1, 1)
            route(1)
            pe.wait_ge(s["weightT_sb"], 1)
            pe.wait_ge(s["first_pick"], 1)
            gather_first(pe, 0)
            place_tokens(1)
            pe.wait_ge(s["first_pick"], 2)
            gather_first(pe, 1).then_inc(rowsT_ps, 1)

            def expert(e, parity, w1_round, first=False, last=False):
                if not first:
                    pe.wait_ge(s["bias_ok"], e + 1)
                    up_bias(pe)
                pe.wait_ge(hTe_ok, e + 1)
                for k in range(W1_CHUNKS):
                    pe.wait_ge(w1_in[parity][k], w1_round * 16)
                    mm = up(pe, w1_slot(parity, k), k, bias_first=not first)
                    if k < W1_CHUNKS - 1:
                        mm.then_inc(w1_used, 1)
                if first:
                    pe.wait_ge(s["bias_ok"], 1)
                    mm = up_bias(pe, first=False)
                mm.then_inc(gemm1, 1)
                if first:
                    transpose_weight(1)
                else:
                    pe.wait_ge(out_ok, e)
                    pe.wait_ge(out2_ok, e)
                    if parity == 0:
                        scatter(pe, slice(0, P))
                pe.wait_ge(put_ok, e + 1)
                transpose_put(pe).then_inc(put_ps, 1)
                if last:
                    scatter(pe, halves(0))
                if not last:
                    pe.wait_ge(pick_ok, e + 1)
                    for tt in range(TT):
                        mm = gather(pe, tt)
                    mm.then_inc(gathered, 1)
                if first:
                    pe.wait_ge(s["weightT_sb"], 2)
                    pe.wait_ge(b2_in, 16)
                    for j in range(2 * TT):
                        start_acc(j)
                pe.wait_ge(glu_ok, e + 1)
                transpose_act(pe).then_inc(actT_ps, 1)
                if not last:
                    pe.wait_ge(rows_ok, e + 1)
                    transpose_rows(pe).then_inc(rowsT_ps, 1)
                pe.wait_ge(put_sb, e + 1)
                pe.wait_ge(actT_sb, e + 1)
                for c in range(W2_CHUNKS):
                    pe.wait_ge(w2_in[c], e * 16 + 16)
                    mm = down(pe, w2_slot(c), c)
                    if c < W2_CHUNKS - 1:
                        mm.then_inc(w2_used, 1)
                mm.then_inc(gemm2, 1)

            expert(0, 0, 1, first=True)
            with pe.Fori(0, E // 2 - 1) as i:
                expert(2 * i + 1, 1, i + 1)
                expert(2 * i + 2, 0, i + 2)
            expert(E - 1, 1, E // 2, last=True)
            pe.wait_ge(out_ok, E)
            pe.wait_ge(out2_ok, E)
            scatter(pe, halves(1), acc_done)

            pe.wait_ge(s["most_ok"], 1)
            most_reg = pe.value_load(most_i[0:1, 0:1], min_val=0, max_val=T)
            with pe.If(most_reg > FIRST_SLOTS):
                with pe.Fori(0, PASSES * E) as n:
                    pe.wait_ge(f_pick, n + 1)
                    transpose_put(pe)
                    for tt in range(TT):
                        mm = gather(pe, tt)
                    mm.then_inc(f_ps, 1)
                    pe.wait_ge(f_rows, n + 1)
                    transpose_rows(pe).then_inc(f_rowsT, 1)
                    pe.wait_ge(f_hT, n + 1)
                    up_bias(pe)
                    pe.wait_ge(f_w, n * (16 * PASS_DMAS) + 16 * PASS_DMAS)
                    for k in range(W1_CHUNKS):
                        mm = up(pe, w1_slot(0, k), k)
                    mm.then_inc(f_g1, 1)
                    pe.wait_ge(f_glu, n + 1)
                    transpose_act(pe).then_inc(f_actT, 1)
                    pe.wait_ge(f_actTs, n + 1)
                    for c in range(W2_CHUNKS):
                        mm = down(pe, w2_slot(c), c)
                    mm.then_inc(f_g2, 1)
                    pe.wait_ge(f_out, n * 2 + 2)
                    scatter(pe, halves(0), acc_done)


_INS = ["x", "attn_norm_g", "w_in", "q_norm_g", "k_norm_g", "pool_w", "pool_b", "pool_scale", "w_branch_attn",
        "w_branch_pool", "w_out", "ffn_norm_g", "router_w", "router_b", "expert_w1", "expert_b1", "expert_w2",
        "expert_b2"]
_OUTS = [((1, 256, 1024), "float32")]


def kernel(**inputs):
    import numpy as _np
    import concourse.bacc as _bacc
    from concourse import mybir as _mybir
    from concourse.bass_utils import run_bass_kernel_spmd as _run

    nc = _bacc.Bacc("TRN2", target_bir_lowering=False, num_devices=1)
    arrays, args = {}, []
    for name in _INS:
        a = _np.ascontiguousarray(inputs[name])
        arrays[f"in_{name}_dram"] = a
        args.append(nc.dram_tensor(f"in_{name}_dram", a.shape, _mybir.dt.from_np(a.dtype), kind="ExternalInput").ap())
    for i, (shape, dtype) in enumerate(_OUTS):
        dt = _mybir.dt.from_np(_np.dtype(dtype))
        args.append(nc.dram_tensor(f"out_{i}_dram", shape, dt, kind="ExternalOutput").ap())
    block_kernel(nc, *args)
    r = _run(nc, [arrays], core_ids=[0])
    return r.results[0]["out_0_dram"]
```
